# Optimizing a Trainium2 kernel written in Bass

```python
import math
import jax, jax.numpy as jnp
from jax import lax
import numpy as np

D_MODEL = 1024
BATCH = 1
SEQ = 1024
DEPTH = 1

CHUNK = 64
N_META = 16
Q_BLOCK = 128
LEAD = Q_BLOCK * ((N_META + Q_BLOCK - 1) // Q_BLOCK)
PAD = LEAD - N_META

MIX = D_MODEL
D_MLSTM = MIX // 2
D_SB = MIX - D_MLSTM
MLSTM_HEADS = 4
MLSTM_DH = D_MLSTM // MLSTM_HEADS
SB_HEADS = 8
SB_DH = D_SB // SB_HEADS
CONV_W = 4
FORGET_BIAS_LO = 3.0
FORGET_BIAS_HI = 6.0

PEER_HEADS = 8
N_KEYS = 128
N_EXPERTS = N_KEYS * N_KEYS
PEER_TOPK = 16
PEER_QDIM = 256
PEER_HALF = PEER_QDIM // 2
TOK_BLOCK = 128

EPS = 1e-6
D_IN_PROJ = 3 * D_MLSTM + 2 * MLSTM_HEADS + 3 * D_SB

kernel_name = 'hybrid_mlstm_stickbreak_peer'

def _split_points():
    sizes = (D_MLSTM, D_MLSTM, D_MLSTM, MLSTM_HEADS, MLSTM_HEADS, D_SB, D_SB, D_SB)
    return [int(s) for s in np.cumsum(sizes)[:-1]]

def rmsnorm(x, g):
    xf = x.astype(jnp.float32)
    y = xf * lax.rsqrt(jnp.mean(xf * xf, axis=-1, keepdims=True) + EPS)
    return (y * g.astype(jnp.float32)).astype(x.dtype)

def mlstm_mixer(u, v, o_pre, i_pre, f_pre, conv_w, conv_b, w_q, w_k, b_i, b_f, skip, gn_g, valid):
    B, L, _ = u.shape
    H, dh = MLSTM_HEADS, MLSTM_DH
    f32 = jnp.float32
    u = jnp.where(valid[None, :, None], u, jnp.zeros_like(u))
    c = lax.conv_general_dilated(u, conv_w[:, None, :].astype(u.dtype), window_strides=(1,),
                                 padding=[(CONV_W - 1, 0)], dimension_numbers=('NWC', 'WIO', 'NWC'),
                                 feature_group_count=D_MLSTM) + conv_b
    c = jax.nn.silu(c)
    ch = c.reshape(B, L, H, dh)
    q = jnp.einsum('blhd,hde->blhe', ch, w_q).astype(f32)
    k = (jnp.einsum('blhd,hde->blhe', ch, w_k) * (dh ** -0.5)).astype(f32)
    vv = v.reshape(B, L, H, dh).astype(f32)
    vmask = valid[None, :, None]
    logi = jnp.where(vmask, (i_pre + b_i).astype(f32), -jnp.inf)
    logf = jnp.where(vmask, jax.nn.log_sigmoid((f_pre + b_f).astype(f32)), 0.0)

    NC = L // CHUNK
    def chunk_vec(t):
        return t.reshape(B, NC, CHUNK, H, dh).transpose(1, 0, 3, 2, 4)
    def chunk_gate(t):
        return t.reshape(B, NC, CHUNK, H).transpose(1, 0, 3, 2)
    tril = jnp.tril(jnp.ones((CHUNK, CHUNK), dtype=bool))

    def step(carry, xs):
        C, n, m = carry
        qc, kc, vc, li, lf = xs
        b = jnp.cumsum(lf, axis=-1)
        D = b[..., :, None] - b[..., None, :] + li[..., None, :]
        D = jnp.where(tril, D, -jnp.inf)
        inter = b + m[..., None]
        m_t = jnp.maximum(inter, jnp.max(D, axis=-1))
        w_intra = jnp.exp(D - m_t[..., None])
        w_inter = jnp.exp(inter - m_t)
        s = jnp.einsum('bhtd,bhsd->bhts', qc, kc) * w_intra
        num = w_inter[..., None] * jnp.einsum('bhed,bhtd->bhte', C, qc) + jnp.einsum('bhts,bhse->bhte', s, vc)
        den = w_inter * jnp.einsum('bhd,bhtd->bht', n, qc) + jnp.sum(s, axis=-1)
        h = num / jnp.maximum(jnp.abs(den), jnp.exp(-m_t))[..., None]
        bL = b[..., -1]
        g = bL[..., None] - b + li
        m_new = jnp.maximum(bL + m, jnp.max(g, axis=-1))
        decay = jnp.exp(bL + m - m_new)
        w = jnp.exp(g - m_new[..., None])
        C_new = decay[..., None, None] * C + jnp.einsum('bhs,bhse,bhsd->bhed', w, vc, kc)
        n_new = decay[..., None] * n + jnp.einsum('bhs,bhsd->bhd', w, kc)
        return (C_new, n_new, m_new), h

    init = (jnp.zeros((B, H, dh, dh), f32), jnp.zeros((B, H, dh), f32), jnp.zeros((B, H), f32))
    _, hs = lax.scan(step, init, (chunk_vec(q), chunk_vec(k), chunk_vec(vv), chunk_gate(logi), chunk_gate(logf)))
    h = hs.transpose(1, 0, 3, 2, 4).reshape(B, L, H, dh)
    h = h * jax.nn.sigmoid(o_pre.astype(f32)).reshape(B, L, H, dh)
    mu = jnp.mean(h, axis=-1, keepdims=True)
    var = jnp.mean(jnp.square(h - mu), axis=-1, keepdims=True)
    hn = ((h - mu) * lax.rsqrt(var + EPS)).reshape(B, L, D_MLSTM)
    out = hn * gn_g.astype(f32) + skip.astype(f32) * c.astype(f32)
    return out.astype(u.dtype)

def stick_breaking_mixer(q, k, v, norm_g, valid):
    B, L, _ = q.shape
    H, dh = SB_HEADS, SB_DH
    f32 = jnp.float32
    qh = (q.reshape(B, L, H, dh).transpose(0, 2, 1, 3) * (dh ** -0.5)).astype(f32)
    kh = k.reshape(B, L, H, dh).transpose(0, 2, 1, 3).astype(f32)
    vh = v.reshape(B, L, H, dh).transpose(0, 2, 1, 3).astype(f32)
    spos = jnp.arange(L)

    def block(bi):
        qb = lax.dynamic_slice_in_dim(qh, bi * Q_BLOCK, Q_BLOCK, axis=2)
        z = jnp.einsum('bhtd,bhsd->bhts', qb, kh)
        tpos = bi * Q_BLOCK + jnp.arange(Q_BLOCK)
        mask = (spos[None, :] < tpos[:, None]) & valid[None, :]
        lneg = jnp.where(mask, jax.nn.log_sigmoid(-z), 0.0)
        rexcl = lax.cumsum(lneg, axis=3, reverse=True) - lneg
        A = jnp.where(mask, jnp.exp(jax.nn.log_sigmoid(z) + rexcl), 0.0)
        return jnp.einsum('bhts,bhsd->bhtd', A, vh)

    o = lax.map(block, jnp.arange(L // Q_BLOCK))
    o = o.transpose(1, 2, 0, 3, 4).reshape(B, H, L, dh).transpose(0, 2, 1, 3)
    o = o * lax.rsqrt(jnp.mean(o * o, axis=-1, keepdims=True) + EPS)
    return (o.reshape(B, L, D_SB) * norm_g.astype(f32)).astype(q.dtype)

def peer_ffn(n, w_query, sub_keys, expert_u, expert_v):
    B, L, D = n.shape
    T, Hh, K = TOK_BLOCK, PEER_HEADS, PEER_TOPK
    xb = n.reshape(B * L // T, T, D)

    def block(xt):
        q = (xt @ w_query).reshape(T, Hh, 2, PEER_HALF)
        s = jnp.einsum('thpc,pnc->thpn', q, sub_keys).astype(jnp.float32)
        sv, si = lax.top_k(s, K)
        cand = (sv[:, :, 0, :, None] + sv[:, :, 1, None, :]).reshape(T, Hh, K * K)
        cidx = (si[:, :, 0, :, None] * N_KEYS + si[:, :, 1, None, :]).reshape(T, Hh, K * K)
        fv, fi = lax.top_k(cand, K)
        eidx = jnp.take_along_axis(cidx, fi, axis=-1)
        g = jax.nn.softmax(fv, axis=-1)
        ue = expert_u[eidx]
        ve = expert_v[eidx]
        act = jax.nn.gelu(jnp.einsum('td,thkd->thk', xt, ue).astype(jnp.float32), approximate=False)
        return jnp.einsum('thk,thkd->td', (g * act).astype(xt.dtype), ve)

    return lax.map(block, xb).reshape(B, L, D)

def setup_inputs(seed: int = 0) -> dict:
    key = jax.random.key(seed)
    ks = jax.random.split(key, 20)
    f32 = jnp.float32
    def nrm(k, shape, scale):
        return jax.random.normal(k, shape, f32) * scale
    H, dh = MLSTM_HEADS, MLSTM_DH
    return {
        'x': nrm(ks[0], (BATCH, SEQ, D_MODEL), 1.0),
        'meta': nrm(ks[1], (N_META, D_MODEL), 1.0),
        'norm_mix_g': 1.0 + nrm(ks[2], (DEPTH, D_MODEL), 0.02),
        'w_in': nrm(ks[3], (DEPTH, D_MODEL, D_IN_PROJ), D_MODEL ** -0.5),
        'conv_w': nrm(ks[4], (DEPTH, CONV_W, D_MLSTM), CONV_W ** -0.5),
        'conv_b': nrm(ks[5], (DEPTH, D_MLSTM), 0.02),
        'w_qm': nrm(ks[6], (DEPTH, H, dh, dh), dh ** -0.5),
        'w_km': nrm(ks[7], (DEPTH, H, dh, dh), dh ** -0.5),
        'b_i': nrm(ks[8], (DEPTH, H), 0.1),
        'b_f': jnp.linspace(FORGET_BIAS_LO, FORGET_BIAS_HI, H, dtype=f32)[None, :] + nrm(ks[9], (DEPTH, H), 0.01),
        'mlstm_skip': 1.0 + nrm(ks[10], (DEPTH, D_MLSTM), 0.02),
        'mlstm_gn_g': 1.0 + nrm(ks[11], (DEPTH, D_MLSTM), 0.02),
        'sb_norm_g': 1.0 + nrm(ks[12], (DEPTH, D_SB), 0.02),
        'w_out': nrm(ks[13], (DEPTH, MIX, D_MODEL), MIX ** -0.5),
        'norm_ffn_g': 1.0 + nrm(ks[14], (DEPTH, D_MODEL), 0.02),
        'w_query': nrm(ks[15], (DEPTH, D_MODEL, PEER_HEADS * PEER_QDIM), D_MODEL ** -0.5),
        'sub_keys': nrm(ks[16], (DEPTH, 2, N_KEYS, PEER_HALF), PEER_HALF ** -0.5),
        'expert_u': nrm(ks[17], (DEPTH, N_EXPERTS, D_MODEL), D_MODEL ** -0.5),
        'expert_v': nrm(ks[18], (DEPTH, N_EXPERTS, D_MODEL), 0.5),
        'norm_final_g': 1.0 + nrm(ks[19], (D_MODEL,), 0.02),
    }

def reference(x, meta, norm_mix_g, w_in, conv_w, conv_b, w_qm, w_km, b_i, b_f, mlstm_skip, mlstm_gn_g,
              sb_norm_g, w_out, norm_ffn_g, w_query, sub_keys, expert_u, expert_v, norm_final_g):
    B, S, D = x.shape
    lead = jnp.concatenate([jnp.zeros((B, PAD, D), x.dtype),
                            jnp.broadcast_to(meta.astype(x.dtype)[None], (B, N_META, D))], axis=1)
    h = jnp.concatenate([lead, x], axis=1)
    L = S + LEAD
    valid = jnp.arange(L) >= PAD
    splits = _split_points()
    for l in range(DEPTH):
        n = rmsnorm(h, norm_mix_g[l])
        proj = n @ w_in[l]
        u, vm, o_pre, i_pre, f_pre, qs, ks_, vs = jnp.split(proj, splits, axis=-1)
        ym = mlstm_mixer(u, vm, o_pre, i_pre, f_pre, conv_w[l], conv_b[l], w_qm[l], w_km[l],
                         b_i[l], b_f[l], mlstm_skip[l], mlstm_gn_g[l], valid)
        ys = stick_breaking_mixer(qs, ks_, vs, sb_norm_g[l], valid)
        h = h + jnp.concatenate([ym, ys], axis=-1) @ w_out[l]
        n = rmsnorm(h, norm_ffn_g[l])
        h = h + peer_ffn(n, w_query[l], sub_keys[l], expert_u[l], expert_v[l])
    return rmsnorm(h[:, LEAD:], norm_final_g)


_drawn_inputs = setup_inputs


def setup_inputs(seed=0):
    import zlib

    import numpy as np

    out = dict(_drawn_inputs(seed))
    spreads = {}
    factors = {'b_i': 64.0,
     'mlstm_skip': 61.434,
     'mlstm_gn_g': 52.858,
     'sb_norm_g': 38.993,
     'norm_final_g': 22.595,
     'norm_ffn_g': 19.103}
    for name, (base, spread) in spreads.items():
        noise = np.random.default_rng([zlib.crc32(name.encode()), seed]).standard_normal(out[name].shape)
        drawn = base * np.exp(spread * noise) if base else spread * noise
        out[name] = __import__('jax').numpy.asarray(drawn.astype(out[name].dtype))
    for name, factor in factors.items():
        out[name] = (out[name] * factor).astype(out[name].dtype)
    return out
```

```python
from contextlib import ExitStack

import concourse.bass as bass
from concourse import mybir

F32 = mybir.dt.float32
BF16 = mybir.dt.bfloat16
I32 = mybir.dt.int32
U32 = mybir.dt.uint32
ALU = mybir.AluOpType
ACT = mybir.ActivationFunctionType
AX_X = mybir.AxisListType.X

P = 128
D = 1024
KC = D // P
SEQ = 1024
N_META = 16
TILES = (P + SEQ) // P
LAST = TILES - 1
MH, MD = 4, 128
SH, SD = 8, 64
SHP = SH // 2
MIX = MH * MD
CONV = 4
D_IN = 6 * MIX + 2 * MH
PH, TOPK, NKEY = 8, 16, 128
NJ = PH * TOPK
EPS = 1e-6
NEG = -1e30
LOWEST = -3.4e38

GROUP = 8
GROUPS = NJ // GROUP
RING = 4
PRE, POST = 2, 5
FILLS = 11
N_CONSTS = 6
MIDDLE = GROUPS - PRE - POST


def units_before(T):
    return (T * T + T - 2) // 2


def wait(eng, sem, value):
    if isinstance(value, int) and value <= 0:
        return
    eng.wait_ge(sem, value)


def diagonal(i):
    return isinstance(i, int) and i == 0


class Links:

    def __init__(self, eng, sem, per):
        self.eng, self.sem, self.per, self.base, self.k = eng, sem, per, 0, per

    def at(self, turn):
        assert self.k == self.per, (self.k, self.per)
        self.base, self.k = turn * self.per, 0

    def __call__(self, ins):
        self.k += 1
        ins.then_inc(self.sem, 1)
        self.eng.wait_ge(self.sem, self.base + self.k)


def program(nc, xT, xn_in, w_in, w_out, w_query, sub_t, mlstm_w, gain_cols, g_ffn, g_final,
            gate_bias, expert_u, expert_v, out):
    with ExitStack() as ctx:
        def sb(name, shape, dt=F32):
            return ctx.enter_context(nc.sbuf_tensor(name, shape, dt))

        def sem(name):
            return ctx.enter_context(nc.semaphore(name))

        mix_dram = nc.dram_tensor("mix_dram", (TILES, P, 4 * MIX), F32).ap()
        kv_dram = nc.dram_tensor("kv_dram", (TILES, P, 2 * MIX), F32).ap()
        top_dram = nc.dram_tensor("top_dram", (MH, TILES * P), F32).ap()
        res_dram = nc.dram_tensor("res_dram", (TILES, P, D), F32).ap()

        weights = sb("weights", [P, KC * D_IN])
        w_in_sb = weights[:, :].rearrange("p (k n) -> p k n", k=KC)
        w_out_sb = weights[:, 0:KC * D].rearrange("p (k n) -> p k n", k=KC)
        w_q_sb = weights[:, KC * D:3 * KC * D].rearrange("p (k n) -> p k n", k=KC)

        sizes = {}
        top = 0
        for name, n in (("ring_u", RING * D), ("ring_v", RING * D), ("arena", 3080), ("keys", MIX),
                        ("vals", MIX), ("cso", 3 * MIX), ("vx", MH * (MD + 1))):
            sizes[name] = (top, top + n)
            top += n
        work = sb("work", [P, top])

        def part(name):
            a, b = sizes[name]
            return work[:, a:b]

        ring_u = part("ring_u").rearrange("p (s d) -> p s d", s=RING)
        ring_v = part("ring_v").rearrange("p (s d) -> p s d", s=RING)
        arena = part("arena")
        keys = part("keys").rearrange("p (c s) -> p c s", c=SHP)
        vals = part("vals").rearrange("p (h d) -> p h d", h=SH)
        cso = part("cso").rearrange("p (a n) -> p a n", a=3)
        cT = cso[:, 0, :].rearrange("p (h t) -> p h t", h=MH)
        so = cso[:, 1, :].rearrange("p (h e) -> p h e", h=MH)
        qsT = cso[:, 2, :].rearrange("p (c t) -> p c t", c=SHP)
        vx = part("vx").rearrange("p (h e) -> p h e", h=MH)

        cut = [0]

        def take(n):
            a = cut[0]
            cut[0] += n
            return work[:, a:a + n]

        xT_sb = [take(D).rearrange("p (k t) -> p k t", k=KC) for _ in range(2)]
        nT = [take(D).rearrange("p (k t) -> p k t", k=KC) for _ in range(2)]
        sqT = take(D).rearrange("p (k t) -> p k t", k=KC)
        stage = [take(6 * MIX) for _ in range(2)]
        ucat = take(MH * (P + 3)).rearrange("p (h t) -> p h t", h=MH)
        conv = take(MIX).rearrange("p (h t) -> p h t", h=MH)
        sig = take(MIX).rearrange("p (h t) -> p h t", h=MH)
        rsT = [take(P) for _ in range(2)]
        assert cut[0] <= top
        cut[0] = 0
        W36 = TILES * MH
        lf = take(W36)
        tmp36 = take(W36)
        li = take(W36)
        rows_a = take(TILES * P)[0:MH, :]
        rows_b = take(TILES * P)[0:MH, :]
        rows_M = take(TILES * P)[0:MH, :]
        rows_wi = take(TILES * P)[0:MH, :]
        rows_em = take(TILES * P)[0:MH, :]
        rows_ws = take(TILES * P)[0:MH, :]
        m_row = take(TILES + 1)[0:MH, :]
        dec_row = take(TILES)[0:MH, :]
        dec_blk = take(W36)[0:MH, :]

        def at(a, n):
            return arena[:, a:a + n]

        q_m = at(0, 512).rearrange("p (h t) -> p h t", h=MH)
        k_m = at(512, 512).rearrange("p (h t) -> p h t", h=MH)
        kw = at(1024, 512).rearrange("p (h e) -> p h e", h=MH)
        wexp = at(1536, 512).rearrange("p (h t) -> p h t", h=MH)
        inter = at(2048, 516).rearrange("p (h e) -> p h e", h=MH)
        nd = at(2564, 516).rearrange("p (h e) -> p h e", h=MH)
        skip_c = q_m
        hb = k_m
        hsq = at(2048, 512).rearrange("p (h e) -> p h e", h=MH)
        zl = [at(512 * i, 512) for i in range(2)]
        sp_ = [at(1024 + 512 * i, 512) for i in range(2)]
        later = [at(2048 + 512 * i, 512) for i in range(2)]
        n2T = at(0, 1024).rearrange("p (k t) -> p k t", k=KC)
        osq = at(0, 512)
        on = at(512, 512)
        qp = [at(1024 + 512 * i, 512).rearrange("p (c t) -> p c t", c=4) for i in range(2)]
        arena_qp = at(1024, 1024)
        hx = at(2048, 1024)

        n2_next = sb("n2_next", [P, D])
        xs = sb("xs", [P, D])
        g_ffn_b = sb("g_ffn_b", [P, D])
        g_fin_b = sb("g_fin_b", [P, D])
        y_res = sb("y_res", [P, D])
        w_qk = sb("w_qk", [P, 2, MH, MD])
        state = sb("state", [P, MH, MD + 1])
        yT = sb("yT", [P, KC, P])
        chosen = sb("chosen", [P, SEQ // P * NJ], I32)
        idx_u = [sb(f"idx_u{i}", [P, GROUP], I32) for i in range(2)]
        idx_v = [sb(f"idx_v{i}", [P, GROUP], I32) for i in range(2)]
        gate_next = sb("gate_next", [P, PH, TOPK])
        gate_now = sb("gate_now", [P, NJ])
        dots = sb("dots", [P, NJ])
        dots8 = sb("dots8", [P, GROUP])
        wgt = sb("wgt", [P, NJ])
        wgt8 = sb("wgt8", [P, GROUP])
        diag = sb("diag", [P, 4, P])
        ident = sb("ident", [P, P])
        ident_h = sb("ident_h", [P, P], BF16)
        neg_m = sb("neg_m", [P, P], BF16)
        neg_s = sb("neg_s", [P, P], BF16)
        before = sb("before", [P, P])
        neg_tri = sb("neg_tri", [P, P])
        ones = sb("ones", [P, P])
        neg_ones = sb("neg_ones", [P, P])
        tri = sb("tri", [P, P])
        subT = sb("subT", [P, 2, NKEY])
        m_top = sb("m_top", [MH, P])
        m_blk = sb("m_blk", [MH, MH, P])
        neg_blk = sb("neg_blk", [MH, MH, P])
        cols = sb("cols", [P, 5, W36])
        now = sb("now", [P, 5, MH])
        graw = sb("graw", [P, TILES, 2 * MH])
        gains = sb("gains", [P, KC + 3 * MH + MH * CONV + MH])
        g_mix = gains[:, 0:8]
        gn_g = gains[:, 8:12]
        skip_g = gains[:, 12:16]
        sb_g = gains[:, 16:20]
        conv_w = gains[:, 20:36]
        conv_b = gains[:, 36:40]
        gbias = sb("gbias", [P, 2 * MH])
        eps = sb("eps", [P, 1])
        one = sb("one", [P, 1])
        valid = sb("valid", [P, 1])
        invalid = sb("invalid", [P, 1])
        small = sb("small", [P, 48])
        den, mean, var, rstd = (small[:, 4 * i:4 * i + 4] for i in range(4))
        oss, ors = small[:, 16:24], small[:, 24:32]
        hss, hrs, yss, yrs = (small[:, 32 + i:33 + i] for i in range(4))
        srt = sb("srt", [P, 2, TOPK])
        sri = sb("sri", [P, 2, TOPK], U32)
        rest = sb("rest", [P, 256])
        cand = sb("cand", [P, TOPK, TOPK])
        best = sb("best", [P, PH, TOPK])
        pos = sb("pos", [P, TOPK], U32)
        half = sb("half", [P, 2, TOPK], U32)
        iota16 = sb("iota16", [P, TOPK])
        iota_i = sb("iota_i", [P, TOPK], I32)
        sel = sb("sel", [P, 2, TOPK])
        gsum = sb("gsum", [P, 2, PH])

        acc = ctx.enter_context(nc.psum_tensor("acc", [P, 2, 512], F32))
        bank = [None, None] + [ctx.enter_context(nc.psum_tensor(f"bank{i}", [P, 512], F32)) for i in range(2, 8)]

        def b4(i):
            return bank[i][:, :].rearrange("p (h t) -> p h t", h=4)

        def b2(i):
            return bank[i][:, 0:2 * (MD + 1)].rearrange("p (h e) -> p h e", h=2)

        consts_in = sem("consts_in")
        fill = sem("fill")
        fills = sem("fills")
        COLS = [("u", 0, MIX), ("ks", 2056, MIX), ("qs", 1544, MIX), ("v", 512, MIX),
                ("so", 1024, MIX), ("vs", 2568, MIX), ("gates", 1536, 2 * MH)]
        w_landed = {n: sem(f"w_landed_{n}") for n, _, _ in COLS}
        x_landed = [sem(f"x_landed{i}") for i in range(2)]
        squared, summed, rs_ready, n_ready = sem("squared"), sem("summed"), sem("rs_ready"), sem("n_ready")
        unit_done = {n: sem(f"{n}_done") for n, _, _ in COLS}
        unit_taken = {n: sem(f"{n}_taken") for n, _, _ in COLS}
        conv_ready, conv_exp, hist_moved, so_exp = sem("conv_ready"), sem("conv_exp"), sem("hist_moved"), sem("so_exp")
        staged_act, staged_dve = sem("staged_act"), sem("staged_dve")
        stored = [sem(f"stored{i}") for i in range(2)]
        act_p, dve_p = sem("act_p"), sem("dve_p")
        gate_in, gate_pe, gate_act, gate_dve, rows_ready, top_ready, top_stored, gates_ready = (
            sem("gate_in"), sem("gate_pe"), sem("gate_act"), sem("gate_dve"), sem("rows_ready"), sem("top_ready"),
            sem("top_stored"), sem("gates_ready"))
        w2_landed = sem("w2_landed")
        mix_in = sem("mix_in")
        now_ready, m_blk_ready = sem("now_ready"), sem("m_blk_ready")
        qk_done, qk_copied, kw_ready = sem("qk_done"), sem("qk_copied"), sem("kw_ready")
        se_done, wexp_ready, p_ready = sem("se_done"), sem("wexp_ready"), sem("p_ready")
        hh_done, dstate_done, inter_ready, state_ready = (
            sem("hh_done"), sem("dstate_done"), sem("inter_ready"), sem("state_ready"))
        var_ready, rstd_ready, hn_ready, hnT_done, skip_ready, ym_ready = (
            sem("var_ready"), sem("rstd_ready"), sem("hn_ready"), sem("hnT_done"), sem("skip_ready"), sem("ym_ready"))
        k_in, v_in = sem("k_in"), sem("v_in")
        z_done, ln_ready, sp_ready, s_done, later_ready, a_ready, av_done = (
            sem("z_done"), sem("ln_ready"), sem("sp_ready"), sem("s_done"),
            sem("later_ready"), sem("a_ready"), sem("av_done"))
        osq_ready, oss_ready, ors_ready, on_ready, onT_done, ys_ready = (
            sem("osq_ready"), sem("oss_ready"), sem("ors_ready"), sem("on_ready"), sem("onT_done"), sem("ys_ready"))
        x_in, mixed, h_ready, h_stored, hrs_ready, n2_ready, n2T_done, n2T_copied = (
            sem("x_in"), sem("mixed"), sem("h_ready"), sem("h_stored"), sem("hrs_ready"), sem("n2_ready"),
            sem("n2T_done"), sem("n2T_copied"))
        qp_done, qp_copied, scores_done, scores_read, idx_ready, soft_in, soft_exp = (
            sem("qp_done"), sem("qp_copied"), sem("scores_done"), sem("scores_read"), sem("idx_ready"),
            sem("soft_in"), sem("soft_exp"))
        dve_m, dve_s, dve_t, dve_e, dve_g = sem("dve_m"), sem("dve_s"), sem("dve_t"), sem("dve_e"), sem("dve_g")
        act_f, act_s, act_o, act_h, act_y = sem("act_f"), sem("act_s"), sem("act_o"), sem("act_h"), sem("act_y")
        dve_turn, act_turn, pool_turn, sp_turn = sem("dve_turn"), sem("act_turn"), sem("pool_turn"), sem("sp_turn")
        u_landed = [sem(f"u_landed{i}") for i in range(RING)]
        v_landed = [sem(f"v_landed{i}") for i in range(RING)]
        u_free, v_free = sem("u_free"), sem("v_free")
        diag_ready, idx_u_copied, idx_v_copied = sem("diag_ready"), sem("idx_u_copied"), sem("idx_v_copied")
        xs_ready = sem("xs_ready")
        dots_moved, wgt_moved = sem("dots_moved"), sem("wgt_moved")
        gelu_ready, wgt_ready = sem("gelu_ready"), sem("wgt_ready")
        res_in, acc_read, yrs_ready, y_ready, out_stored = (
            sem("res_in"), sem("acc_read"), sem("yrs_ready"), sem("y_ready"), sem("out_stored"))

        block = ctx.enter_context(nc.Block())

        PSUM_OF = {"u": 2, "ks": 3, "qs": 4, "v": 5, "so": 6, "vs": 7}
        gate_psum = acc[:, 0, 0:2 * MH]
        sum_psum = acc[:, 1, 0:P]
        SLOT = {"c": 0, "v": 1, "so": 2, "qs": 3, "ks": 4, "vs": 5}

        def slot(p, name):
            return stage[p][:, SLOT[name] * MIX:(SLOT[name] + 1) * MIX]

        def slot4(p, name):
            return slot(p, name).rearrange("p (h t) -> p h t", h=4)

        def project(eng, tile_step):
            tile_step(0, 0, 0)
            tile_step(1, 1, 0)
            with eng.Fori(1, (TILES - 1) // 2) as k:
                tile_step(2 * k, 0, k)
                tile_step(2 * k + 1, 1, k)
            tile_step(LAST, 0, LAST // 2)

        def tile_of(dram, T):
            return dram[bass.ds(T, 1)].rearrange("a p n -> (a p) n")

        def wide(ap, shape):
            return ap.unsqueeze(len(shape) - 1).broadcast_to(shape)

        @block.sync
        def _(sp):
            def load_x(T, p):
                sp.dma_start(xT_sb[p], xT[:, bass.ds(T * P, P)].rearrange("(k p) t -> p k t", p=P)).then_inc(
                    x_landed[p], 16)

            load_x(0, 0)
            sp.dma_start(gains[:, :], gain_cols).then_inc(consts_in, 16)
            for n, a, w in COLS:
                sp.dma_start(w_in_sb[:, :, a:a + w],
                             w_in.rearrange("(k p) n -> p k n", p=P)[:, :, a:a + w]).then_inc(w_landed[n], 16)
                if n == "u":
                    sp.dma_start(gbias[:, :], gate_bias.broadcast_to([P, 2 * MH])).then_inc(consts_in, 16)
                    load_x(1, 1)
            sp.dma_start(g_ffn_b[:, :], g_ffn.broadcast_to([P, D])).then_inc(consts_in, 16)
            sp.dma_start(g_fin_b[:, :], g_final.broadcast_to([P, D])).then_inc(consts_in, 16)
            sp.dma_start(w_qk[:, :, :, :], mlstm_w).then_inc(consts_in, 16)
            sp.dma_start(subT[:, :, :], sub_t).then_inc(consts_in, 16)

            def store(T, p, more=True):
                sp.wait_ge(staged_act, T + 1)
                sp.wait_ge(staged_dve, T + 1)
                first = isinstance(T, int) and T == 0
                n = 2 * MIX if first else 4 * MIX
                sp.dma_start(tile_of(mix_dram, T)[:, 0:n], stage[p][:, 0:n]).then_inc(stored[p], 16)
                sp.dma_start(tile_of(kv_dram, T), stage[p][:, 4 * MIX:6 * MIX]).then_inc(stored[p], 16)
                if more:
                    sp.wait_ge(n_ready, T + 1)
                    sp.wait_ge(squared, T + 1)
                    load_x(T + 2, p)

            store(0, 0)
            store(1, 1)
            with sp.Fori(1, 3) as k:
                store(2 * k, 0)
                store(2 * k + 1, 1)
            store(6, 0)
            store(7, 1, more=False)
            store(8, 0, more=False)
            sp.wait_ge(unit_done["gates"], TILES)
            sp.dma_start(w_out_sb, w_out.rearrange("(k p) n -> p k n", p=P)).then_inc(w2_landed, 16)
            sp.dma_start(w_q_sb, w_query.rearrange("(k p) n -> p k n", p=P)).then_inc(w2_landed, 16)
            sp.wait_ge(top_ready, 1)
            sp.dma_start(top_dram, rows_M).then_inc(top_stored, 16)
            sp.wait_ge(top_stored, 16)
            sp.wait_ge(stored[0], 32 * 5)
            sp.wait_ge(stored[1], 32 * 4)
            sp.wait_ge(gates_ready, 1)

            def load_mix(T):
                src = tile_of(mix_dram, T)
                lead = isinstance(T, int) and T == 0
                wait(sp, state_ready, T)
                if not lead:
                    wait(sp, ym_ready, T - 1)
                    wait(sp, av_done, units_before(T))
                sp.dma_start(cso[:, 0, :], src[:, 0:MIX]).then_inc(mix_in, 16)
                sp.dma_start(vx[:, :, 0:MD], src[:, MIX:2 * MIX].rearrange("p (h e) -> p h e", h=MH)).then_inc(
                    mix_in, 16)
                if lead:
                    return
                sp.dma_start(cso[:, 1:3, :], src[:, 2 * MIX:4 * MIX].rearrange("p (a n) -> p a n", a=2)).then_inc(
                    mix_in, 16)
                sp.dma_start(m_top[:, :], top_dram[:, bass.ds(T * P, P)]).then_inc(mix_in, 16)

            def load_kv(T, i):
                c = units_before(T) + i
                kb = T - i
                if not isinstance(kb, int):
                    kb = nc.s_assert_within(kb, 0, LAST, skip_runtime_bounds_check_because="i goes from 1 to T")
                src = tile_of(kv_dram, kb)
                wait(sp, z_done, 2 * c)
                sp.sem_inc(sp_turn, 1)
                sp.dma_start(keys, src[:, 0:MIX].rearrange("p (c s) -> p c s", c=SHP)).then_inc(k_in, 16)
                wait(sp, av_done, c)
                sp.dma_start(vals, src[:, MIX:2 * MIX].rearrange("p (h d) -> p h d", h=SH)).then_inc(v_in, 16)

            def load_res(T):
                sp.wait_ge(av_done, units_before(T + 1))
                sp.wait_ge(later_ready, units_before(T + 1))
                sp.dma_start(hx, xn_in[bass.ds(T * P, P), :]).then_inc(x_in, 16)
                sp.wait_ge(h_ready, T)
                sp.dma_start(tile_of(res_dram, T), hx).then_inc(h_stored, 16)

            load_mix(0)
            load_mix(1)
            load_kv(1, 0)
            load_kv(1, 1)
            load_res(1)

            def step(T, front=True, sums=True):
                if sums:
                    wait(sp, out_stored, 16 * (T - 2))
                    sp.wait_ge(h_stored, 16 * (T - 1))
                    sp.dma_start(y_res[:, :], tile_of(res_dram, T - 1)).then_inc(res_in, 16)
                if front:
                    load_mix(T + 1)
                    load_kv(T + 1, 0)
                    with sp.Fori(1, T + 2) as i:
                        load_kv(T + 1, i)
                    load_res(T + 1)
                if sums:
                    sp.wait_ge(y_ready, T - 1)
                    sp.dma_start(out[bass.ds((T - 2) * P, P), :], y_res[:, :]).then_inc(out_stored, 16)

            step(1, sums=False)
            step(2)
            with sp.Fori(3, LAST) as T:
                step(T)
            step(LAST, front=False)
            step(LAST + 1, front=False)
            sp.wait_ge(out_stored, 16 * LAST)
            sp.wait_ge(h_stored, 16 * LAST)

        @block.gpsimd
        def _(pool):
            def select(tile, sign, op, fill_value):
                pool.affine_select(out=tile[:, :], in_=tile[:, :], compare_op=op, fill=fill_value, base=0,
                                   pattern=[[-sign, P]], channel_multiplier=sign).then_inc(fills, 1)

            for tile, value in ((ident, 1.0), (ident_h, 1.0), (neg_m, 0.0), (neg_s, 0.0), (before, 1.0),
                                (neg_tri, -1.0), (ones, 1.0), (neg_ones, -1.0), (tri, 1.0), (valid, 1.0),
                                (invalid, 0.0), (eps, EPS), (one, 1.0)):
                pool.memset(tile[:, :], value)
            pool.memset(neg_blk[:, :, :], -1.0)
            pool.iota(iota_i[:, :], [[1, TOPK]], base=0, channel_multiplier=0)
            pool.memset(state[:, :, :], 0.0).then_inc(fill, 1)
            pool.wait_ge(fill, 1)
            select(ident, 1, ALU.is_equal, 0.0)
            select(ident_h, 1, ALU.is_equal, 0.0)
            select(neg_m, -1, ALU.is_ge, NEG)
            select(neg_s, -1, ALU.is_gt, NEG)
            select(before, -1, ALU.is_gt, 0.0)
            select(neg_tri, 1, ALU.is_ge, 0.0)
            select(tri, -1, ALU.is_ge, 0.0)
            pool.affine_select(out=valid[:, :], in_=valid[:, :], compare_op=ALU.is_ge, fill=0.0,
                               base=-(P - N_META), pattern=[[0, 1]], channel_multiplier=1).then_inc(fills, 1)
            pool.affine_select(out=invalid[:, :], in_=invalid[:, :], compare_op=ALU.is_ge, fill=NEG,
                               base=-(P - N_META), pattern=[[0, 1]], channel_multiplier=1).then_inc(fills, 1)
            pool.affine_select(out=neg_blk[:, :, :], in_=neg_blk[:, :, :], compare_op=ALU.is_equal, fill=0.0,
                               base=0, pattern=[[-1, MH], [0, P]], channel_multiplier=1).then_inc(fills, 1)
            pool.tensor_copy(iota16[:, :], iota_i[:, :]).then_inc(fills, 1)

            def gather(ring, s, landed, free, table, idx, jj, n):
                pool.wait_ge(free, n + 1)
                pool.sem_inc(pool_turn, 1)
                pool.indirect_dma_start(out=ring[:, s, :], out_offset=None, in_=table,
                                        in_offset=bass.IndirectOffsetOnAxis(ap=idx[:, jj:jj + 1], axis=0)
                                        ).then_inc(landed[s], 16)

            def picks(T, g, q, dot, sums):
                a, b = (T - 1) * GROUPS + g, (T - 2) * GROUPS + g
                if dot:
                    pool.wait_ge(idx_ready, (T - 1) * PH + g_head(g, q) + 1)
                    pool.sem_inc(pool_turn, 1)
                    pool.tensor_copy(idx_u[q][:, :], chosen[:, bass.ds((T - 1) * NJ + g * GROUP, GROUP)]).then_inc(
                        idx_u_copied, 1)
                if sums:
                    pool.tensor_copy(idx_v[q][:, :], chosen[:, bass.ds((T - 2) * NJ + g * GROUP, GROUP)]).then_inc(
                        idx_v_copied, 1)
                if dot:
                    pool.wait_ge(idx_u_copied, a + 1)
                if sums:
                    pool.wait_ge(idx_v_copied, b + 1)
                pool.sem_inc(pool_turn, 1)
                for jj in range(GROUP):
                    if dot:
                        gather(ring_u, jj % RING, u_landed, u_free, expert_u, idx_u[q], jj, a * GROUP + jj)
                    if sums:
                        gather(ring_v, jj % RING, v_landed, v_free, expert_v, idx_v[q], jj, b * GROUP + jj)

            def g_head(g, q):
                return (g - q) // 2

            def step(T, dot=True, sums=True):
                with pool.Fori(0, PH) as h:
                    for q in range(2):
                        picks(T, 2 * h + q, q, dot, sums)

            step(1, sums=False)
            with pool.Fori(2, LAST + 1) as T:
                step(T)
            step(LAST + 1, dot=False)

        def expert_step(eng, T, group, hooks, middle, front):
            Tf = T + 1
            for g in range(PRE):
                group(T, g, {jj: hooks[g, jj] for jj in range(GROUP) if (g, jj) in hooks} if front else {}, Tf)
            if front:
                with eng.Fori(1, Tf + 1) as i:
                    group(T, i + (PRE - 1), {jj: (lambda t, f=f: f(t, i)) for jj, f in middle.items()}, Tf)
                with eng.Fori(PRE, PRE + MIDDLE - Tf) as g:
                    group(T, g + Tf, {}, Tf)
            else:
                with eng.Fori(PRE, PRE + MIDDLE) as g:
                    group(T, g, {}, Tf)
            for g in range(PRE + MIDDLE, GROUPS):
                group(T, g, {jj: hooks[g, jj] for jj in range(GROUP) if (g, jj) in hooks} if front else {}, Tf)

        def expert_steps(eng, group, end, begin, hooks, middle):
            def one(T, front, dot, sums):
                begin(T, dot, sums)
                expert_step(eng, T, lambda *a: group(*a, dot=dot, sums=sums), hooks, middle, front)
                end(T, dot, sums)

            one(1, True, True, False)
            one(2, True, True, True)
            with eng.Fori(3, LAST) as T:
                one(T, True, True, True)
            one(LAST, False, True, True)
            one(LAST + 1, False, False, True)

        def in_order(T, hooks, middle):
            for key in sorted(k for k in hooks if k[0] < PRE):
                hooks[key](T)
            for i in range(1, T + 1):
                for jj in sorted(middle):
                    middle[jj](T, i)
            for key in sorted(k for k in hooks if k[0] >= PRE):
                hooks[key](T)

        def both_of(*fs):
            def f(*a):
                for g in fs:
                    g(*a)
            return f

        @block.scalar
        def _(act):
            def copy(out_, in_, scale=1.0):
                return nc.scalar.activation(out_, in_, ACT.Copy, scale=scale)

            act.wait_ge(fills, FILLS)
            act.wait_ge(consts_in, 16 * N_CONSTS)
            Lp = Links(act, act_p, 1)

            def norms(T, p, k):
                act.wait_ge(x_landed[p], 16 * (k + 1))
                wait(act, summed, T)
                nc.scalar.activation(sqT, xT_sb[p], ACT.Square).then_inc(squared, 1)
                act.wait_ge(summed, T + 1)
                wait(act, n_ready, T - 1)
                Lp.at(T)
                Lp(nc.scalar.activation(rsT[p], sum_psum, ACT.Ln, scale=1.0 / D, bias=eps[:, :]))
                nc.scalar.activation(rsT[p], rsT[p], ACT.Exp, scale=-0.5).then_inc(rs_ready, 1)

            def tile_step(T, p, k):
                lead = isinstance(T, int) and T == 0
                wait(act, stored[p], 32 * k)
                act.wait_ge(unit_done["u"], T + 1)
                wait(act, hist_moved, T + 1)
                copy(ucat[:, :, 3:], b4(2)).then_inc(unit_taken["u"], 1)
                if not (isinstance(T, int) and T == LAST):
                    norms(T + 1, 1 - p, k + p)
                if not lead:
                    act.wait_ge(unit_done["qs"], T)
                    copy(slot(p, "qs"), bank[4][:, :], SD ** -0.5).then_inc(unit_taken["qs"], 1)
                    act.wait_ge(unit_done["so"], T)
                    nc.scalar.activation(slot(p, "so"), bank[6][:, :], ACT.Exp, scale=-1.0).then_inc(
                        unit_taken["so"], 1)
                act.wait_ge(conv_ready, T + 1)
                nc.scalar.activation(sig, conv, ACT.Exp, scale=-1.0).then_inc(conv_exp, 1)
                act.wait_ge(unit_done["vs"], T + 1)
                copy(slot(p, "vs"), bank[7][:, :]).then_inc(unit_taken["vs"], 1)
                act.sem_inc(act_turn, 1)
                act.wait_ge(unit_taken["vs"], T + 1)
                act.sem_inc(staged_act, 1)

            norms(0, 0, 0)
            project(act, tile_step)

            act.wait_ge(unit_taken["gates"], TILES)
            act.wait_ge(stored[0], 32 * 5)
            act.wait_ge(stored[1], 32 * 4)
            nc.scalar.activation(tmp36.rearrange("p (t h) -> p t h", t=TILES), graw[:, :, MH:2 * MH],
                                 ACT.Abs).then_inc(gate_act, 1)
            act.wait_ge(gate_act, 1)
            nc.scalar.activation(tmp36, tmp36, ACT.Exp, scale=-1.0).then_inc(gate_act, 1)
            act.wait_ge(gate_act, 2)
            nc.scalar.activation(tmp36, tmp36, ACT.Ln, bias=one[:, :]).then_inc(gate_act, 1)
            act.wait_ge(rows_ready, 1)
            nc.scalar.activation(rows_wi, rows_wi, ACT.Exp)
            nc.scalar.activation(rows_em, rows_em, ACT.Exp, scale=-1.0)
            nc.scalar.activation(rows_ws, rows_ws, ACT.Exp)
            nc.scalar.activation(dec_row, dec_row, ACT.Exp).then_inc(gate_act, 1)

            def copy_qk(T):
                act.wait_ge(qk_done, T + 1)
                copy(q_m, b4(2))
                copy(k_m, b4(3), MD ** -0.5).then_inc(qk_copied, 1)

            def exp_w(T):
                act.wait_ge(se_done, T)
                act.wait_ge(now_ready, T + 1)
                for h in range(MH):
                    last = nc.scalar.activation(wexp[:, h, :], b4(3)[:, h, :], ACT.Exp, bias=now[:, 0, h:h + 1])
                last.then_inc(wexp_ready, 1)

            def scale_inter(T):
                act.wait_ge(hh_done, T)
                for h in range(MH):
                    last = copy(inter[:, h, :], b2(6 + h // 2)[:, h % 2, :], now[:, 1, h:h + 1])
                last.then_inc(inter_ready, 1)

            Lf = Links(act, act_f, 1)

            def rsqrt(out_, in_, n):
                Lf(nc.scalar.activation(out_, in_, ACT.Ln, scale=1.0 / n, bias=eps[:, :]))
                return nc.scalar.activation(out_, out_, ACT.Exp, scale=-0.5)

            def rstd_m(T):
                Lf.at(T - 1)
                act.wait_ge(var_ready, T)
                rsqrt(rstd, var, MD).then_inc(rstd_ready, 1)

            def skip_m(T):
                act.wait_ge(dstate_done, T + 1)
                for h in range(MH):
                    last = copy(skip_c[:, h, :], cT[:, h, :], skip_g[:, h:h + 1])
                last.then_inc(skip_ready, 1)

            Ls = Links(act, act_s, 4)

            def ln_z(T, i):
                c = units_before(T) + i
                Ls.at(c)
                if diagonal(i):
                    act.wait_ge(ym_ready, T)
                wait(act, av_done, c)
                for hg in range(2):
                    act.wait_ge(z_done, 2 * c + hg + 1)
                    Ls(nc.scalar.activation(zl[hg], bank[2 + hg][:, :], ACT.Abs))
                    Ls(nc.scalar.activation(zl[hg], zl[hg], ACT.Exp, scale=-1.0))
                    nc.scalar.activation(zl[hg], zl[hg], ACT.Ln, bias=one[:, :]).then_inc(ln_ready, 1)

            def exp_a(T, i):
                c = units_before(T) + i
                for hg in range(2):
                    act.wait_ge(s_done, 2 * c + hg + 1)
                    act.wait_ge(sp_ready, 2 * c + hg + 1)
                    nc.scalar.activation(zl[hg], bank[2 + hg][:, :], ACT.Exp).then_inc(a_ready, 1)

            def square_o(T):
                act.wait_ge(av_done, units_before(T + 1))
                nc.scalar.activation(osq, bank[5][:, :], ACT.Square).then_inc(osq_ready, 1)

            Lo = Links(act, act_o, 1)

            def rs_o(T):
                act.wait_ge(oss_ready, T)
                Lo.at(T - 1)
                Lo(nc.scalar.activation(ors, oss, ACT.Ln, scale=1.0 / SD, bias=eps[:, :]))
                nc.scalar.activation(ors, ors, ACT.Exp, scale=-0.5).then_inc(ors_ready, 1)

            def copy_ys(T):
                act.wait_ge(onT_done, T)
                for h in range(4):
                    last = copy(yT[:, 4 + h, :], b4(2)[:, h, :], sb_g[:, h:h + 1])
                last.then_inc(ys_ready, 1)

            Lh = Links(act, act_h, 2)

            def rs_h(T):
                act.wait_ge(h_ready, T)
                Lh.at(T - 1)
                Lh(nc.scalar.activation(arena_qp, hx, ACT.Square, accum_out=hss))
                Lh(nc.scalar.activation(hrs, hss, ACT.Ln, scale=1.0 / D, bias=eps[:, :]))
                nc.scalar.activation(hrs, hrs, ACT.Exp, scale=-0.5).then_inc(hrs_ready, 1)

            def copy_n2T(T):
                act.wait_ge(n2T_done, T)
                copy(n2T[:, 0:4, :], b4(2))
                copy(n2T[:, 4:8, :], b4(3)).then_inc(n2T_copied, 1)

            def copy_qp(q4):
                def f(T):
                    act.wait_ge(qp_done, 4 * (T - 1) + q4 + 1)
                    if q4 >= 2:
                        act.wait_ge(scores_done, 4 * (T - 1) + q4 - 1)
                    copy(qp[q4 % 2], b4(4 + q4 % 2)).then_inc(qp_copied, 1)
                return f

            def exp_soft(T):
                act.wait_ge(soft_in, T)
                nc.scalar.activation(gate_next[:, :, :], gate_next[:, :, :], ACT.Exp).then_inc(soft_exp, 1)

            hooks = {(0, 1): copy_qk, (0, 4): exp_w, (0, 7): both_of(scale_inter), (1, 1): rstd_m, (1, 3): skip_m,
                     (1, 5): lambda T: ln_z(T, 0), (1, 7): lambda T: exp_a(T, 0),
                     (11, 0): square_o, (11, 2): rs_o, (11, 4): copy_ys, (12, 2): rs_h, (12, 4): copy_n2T,
                     (12, 6): copy_qp(0), (13, 1): copy_qp(1), (13, 7): copy_qp(2), (14, 5): copy_qp(3),
                     (15, 7): exp_soft}
            middle = {2: ln_z, 5: exp_a}

            in_order(1, hooks, middle)

            def begin(T, dot, sums):
                if sums:
                    act.wait_ge(wgt_ready, T - 1)

            def group(T, g, at_pick, Tf, dot, sums):
                n = ((T - 2) * GROUPS + g) * GROUP
                fixed = isinstance(g, int)
                if sums and not fixed:
                    act.wait_ge(diag_ready, n)
                    act.sem_inc(act_turn, 1)
                    copy(wgt8[:, :], wgt[:, bass.ds(g * GROUP, GROUP)]).then_inc(wgt_moved, 1)
                    act.wait_ge(wgt_moved, (T - 2) * MIDDLE + g - (PRE - 1))
                for jj in range(GROUP):
                    if sums:
                        act.wait_ge(v_free, n + jj + 1)
                        col = wgt[:, g * GROUP + jj:g * GROUP + jj + 1] if fixed else wgt8[:, jj:jj + 1]
                        copy(diag[:, jj % 4, :], ident[:, :], col).then_inc(diag_ready, 1)
                    if jj in at_pick:
                        at_pick[jj](Tf)

            Ly = Links(act, act_y, 2)

            def end(T, dot, sums):
                if dot:
                    act.wait_ge(u_free, RING + T * NJ)
                    act.wait_ge(dots_moved, T * MIDDLE)
                    nc.scalar.activation(dots[:, :], dots[:, :], ACT.Gelu).then_inc(gelu_ready, 1)
                if sums:
                    act.wait_ge(acc_read, T - 1)
                    Ly.at(T - 2)
                    Ly(nc.scalar.activation(diag[:, :, :].bitcast(BF16)[:, :, 0:P * 2].rearrange("p a b -> p (a b)"),
                                            y_res[:, :], ACT.Square, accum_out=yss))
                    Ly(nc.scalar.activation(yrs, yss, ACT.Ln, scale=1.0 / D, bias=eps[:, :]))
                    nc.scalar.activation(yrs, yrs, ACT.Exp, scale=-0.5).then_inc(yrs_ready, 1)

            expert_steps(act, group, end, begin, hooks, middle)

        @block.vector
        def _(dve):
            def TT(out_, a, b, op):
                return nc.vector.tensor_tensor(out_, a, b, op)

            def TS(out_, a, s1, op0, s2=None, op1=None):
                if op1 is None:
                    return nc.vector.tensor_scalar(out_, a, s1, None, op0)
                return nc.vector.tensor_scalar(out_, a, s1, s2, op0, op1)

            def STT(out_, a, s, b, op0, op1):
                return nc.vector.scalar_tensor_tensor(out=out_, in0=a, scalar=s, in1=b, op0=op0, op1=op1)

            nc.vector.memset(ucat[:, :, 0:3], 0.0).then_inc(hist_moved, 1)
            dve.wait_ge(fills, FILLS)
            dve.wait_ge(consts_in, 16 * N_CONSTS)

            def normalise(T, p):
                dve.wait_ge(rs_ready, T + 1)
                wait(dve, unit_done["gates"], T - 1)
                for k in range(KC):
                    last = STT(nT[p][:, k, :], xT_sb[p][:, k, :], g_mix[:, k:k + 1], rsT[p], ALU.mult, ALU.mult)
                last.then_inc(n_ready, 1)

            Lp = Links(dve, dve_p, CONV + 5)

            def tile_step(T, p, k):
                lead = isinstance(T, int) and T == 0
                if not (isinstance(T, int) and T == LAST):
                    normalise(T + 1, 1 - p)
                Lp.at(T)
                dve.wait_ge(unit_taken["u"], T + 1)
                for w in range(CONV):
                    for h in range(MH):
                        c, tap = conv[:, h, :], conv_w[:, h * CONV + w:h * CONV + w + 1]
                        if w == 0:
                            last = TS(c, ucat[:, h, 0:P], tap, ALU.mult, conv_b[:, h:h + 1], ALU.add)
                        else:
                            last = STT(c, ucat[:, h, w:w + P], tap, c, ALU.mult, ALU.add)
                    if w == CONV - 1:
                        last.then_inc(conv_ready, 1)
                        dve.wait_ge(conv_ready, T + 1)
                        dve.sem_inc(dve_p, 1)
                        Lp.k += 1
                    else:
                        Lp(last)
                nc.vector.tensor_copy(ucat[:, :, 0:3], ucat[:, :, P:P + 3]).then_inc(hist_moved, 1)
                wait(dve, stored[p], 32 * k)
                dve.wait_ge(unit_done["ks"], T + 1)
                nc.vector.tensor_copy(slot(p, "ks"), bank[3][:, :]).then_inc(unit_taken["ks"], 1)
                dve.wait_ge(unit_done["v"], T + 1)
                nc.vector.tensor_copy(slot(p, "v"), bank[5][:, :]).then_inc(unit_taken["v"], 1)
                dve.wait_ge(conv_exp, T + 1)
                Lp(TS(sig, sig, 1.0, ALU.add))
                Lp(nc.vector.reciprocal(sig, sig))
                Lp(TT(slot4(p, "c"), conv, sig, ALU.mult))
                if lead:
                    dve.sem_inc(dve_p, 2)
                    Lp.k += 2
                else:
                    dve.wait_ge(unit_taken["so"], T)
                    Lp(TS(slot(p, "so"), slot(p, "so"), 1.0, ALU.add))
                    Lp(nc.vector.reciprocal(slot(p, "so"), slot(p, "so")))
                dve.wait_ge(unit_done["gates"], T + 1)
                TT(graw[:, bass.ds(T, 1), :].rearrange("p a b -> p (a b)"), gate_psum, gbias[:, :],
                   ALU.add).then_inc(unit_taken["gates"], 1)
                dve.wait_ge(unit_taken["gates"], T + 1)
                dve.sem_inc(staged_dve, 1)

            normalise(0, 0)
            project(dve, tile_step)

            dve.wait_ge(stored[0], 32 * 5)
            dve.wait_ge(stored[1], 32 * 4)
            n_link = [0]

            def L(ins):
                n_link[0] += 1
                ins.then_inc(gate_dve, 1)
                dve.wait_ge(gate_dve, n_link[0])

            g9 = graw[:, :, :]

            def v9(ap):
                return ap.rearrange("p (t h) -> p t h", t=TILES)

            L(nc.vector.tensor_copy(v9(li), g9[:, :, 0:MH]))
            L(TS(li[:, 0:MH], li[:, 0:MH], valid[:, :], ALU.mult, invalid[:, :], ALU.add))
            dve.wait_ge(gate_act, 3)
            L(STT(v9(lf), g9[:, :, MH:2 * MH], 0.0, v9(tmp36), ALU.min, ALU.subtract))
            TS(lf[:, 0:MH], lf[:, 0:MH], valid[:, :], ALU.mult).then_inc(gate_in, 1)
            dve.wait_ge(gate_pe, 1)
            L(TT(cols[:, 0, :], li, bank[2][:, 0:W36], ALU.subtract))
            L(nc.vector.tensor_copy(tmp36, bank[2][:, 0:W36]))
            dve.sem_inc(gate_in, 1)
            dve.wait_ge(gate_pe, 2)
            for i in range(3):
                a, b = 512 * i, min(512 * (i + 1), TILES * P)
                L(nc.vector.tensor_copy(rows_a[:, a:b], bank[3 + i][0:MH, 0:b - a]))
            for i in range(3):
                a, b = 512 * i, min(512 * (i + 1), TILES * P)
                L(nc.vector.tensor_copy(rows_b[:, a:b], bank[(6, 7, 2)[i]][0:MH, 0:b - a]))
            L(nc.vector.memset(m_row[:, 0:1], 0.0))
            for T in range(TILES):
                r = rows_a[:, T * P:(T + 1) * P]
                L(nc.vector.tensor_tensor_scan(rows_M[:, T * P:(T + 1) * P], r, r, m_row[:, T:T + 1],
                                               ALU.max, ALU.max))
                e = (T + 1) * P
                L(TT(m_row[:, T + 1:T + 2], rows_b[:, e - 1:e], rows_M[:, e - 1:e], ALU.add))
            dve.sem_inc(top_ready, 1)

            def r3(ap):
                return ap.rearrange("p (t s) -> p t s", t=TILES)

            def spread(ap):
                return wide(ap, [MH, TILES, P])

            M_end = r3(rows_M)[:, :, P - 1]
            TT(r3(rows_wi), spread(m_row[:, 0:TILES]), r3(rows_M), ALU.subtract)
            TT(rows_em, rows_b, rows_M, ALU.add)
            TT(r3(rows_ws), r3(rows_a), spread(M_end), ALU.subtract)
            L(TT(dec_row, m_row[:, 0:TILES], M_end, ALU.subtract))
            dve.sem_inc(rows_ready, 1)
            dve.wait_ge(gate_act, 4)
            L(STT(dec_blk.rearrange("p (t h) -> p t h", t=TILES), wide(dec_row, [MH, TILES, MH]), -1.0,
                  neg_blk[:, :, 0].unsqueeze(1).broadcast_to([MH, TILES, MH]), ALU.mult, ALU.mult))
            dve.sem_inc(gate_in, 1)
            dve.wait_ge(gate_pe, 3)
            L(nc.vector.tensor_copy(cols[:, 1:4, :], bank[3][:, 0:3 * W36].rearrange("p (a b) -> p a b", a=3)))
            L(nc.vector.tensor_copy(cols[:, 4, :], bank[4][:, 0:W36]))
            L(nc.vector.memset(vx[:, :, MD:MD + 1], 1.0))
            dve.sem_inc(gates_ready, 1)

            Lm = Links(dve, dve_m, 9)

            def set_now(T):
                lead = isinstance(T, int) and T == 0
                wait(dve, state_ready, T)
                dve.sem_inc(dve_turn, 1)
                nc.vector.tensor_copy(now[:, :, :], cols[:, :, bass.ds(T * MH, MH)]).then_inc(now_ready, 1)
                dve.wait_ge(now_ready, T + 1)
                dve.wait_ge(mix_in, 32 + 64 * T)
                if not lead:
                    TT(m_blk[:, :, :], m_top[:, :].unsqueeze(1).broadcast_to([MH, MH, P]), neg_blk[:, :, :],
                       ALU.mult).then_inc(m_blk_ready, 1)

            def make_kw(T):
                dve.wait_ge(qk_done, T + 1)
                for h in range(MH):
                    last = TS(kw[:, h, :], b4(4)[:, h, :], MD ** -0.5, ALU.mult, now[:, 3, h:h + 1], ALU.mult)
                last.then_inc(kw_ready, 1)

            def make_p(T):
                dve.wait_ge(wexp_ready, T)
                TT(wexp, b4(2), wexp, ALU.mult).then_inc(p_ready, 1)

            def update_state(T):
                dve.wait_ge(dstate_done, T + 1)
                for h in range(MH):
                    last = STT(state[:, h, :], state[:, h, :], now[:, 4, h:h + 1], b2(2 + h // 2)[:, h % 2, :],
                               ALU.mult, ALU.add)
                last.then_inc(state_ready, 1)

            def make_h(T):
                Lm.at(T - 1)
                dve.wait_ge(inter_ready, T)
                for i in range(2):
                    last = TT(nd[:, 2 * i:2 * i + 2, :], inter[:, 2 * i:2 * i + 2, :], b2(4 + i), ALU.add)
                Lm(last)
                update_state(T)
                Lm(STT(den, nd[:, :, MD], -1.0, nd[:, :, MD], ALU.mult, ALU.max))
                Lm(TT(den, den, now[:, 2, :], ALU.max))
                Lm(nc.vector.reciprocal(den, den))
                for h in range(MH):
                    last = STT(hb[:, h, :], nd[:, h, 0:MD], den[:, h:h + 1], so[:, h, :], ALU.mult, ALU.mult)
                Lm(last)
                Lm(nc.vector.tensor_reduce(mean, hb, AX_X, ALU.add))
                Lm(TS(mean, mean, -1.0 / MD, ALU.mult))
                Lm(TT(hb, hb, wide(mean, [P, MH, MD]), ALU.add))
                Lm(TT(hsq, hb, hb, ALU.mult))
                nc.vector.tensor_reduce(var, hsq, AX_X, ALU.add).then_inc(var_ready, 1)

            def make_hn(T):
                dve.wait_ge(rstd_ready, T)
                TT(hb, hb, wide(rstd, [P, MH, MD]), ALU.mult).then_inc(hn_ready, 1)

            def make_ym(T):
                dve.wait_ge(hnT_done, T)
                dve.wait_ge(skip_ready, T)
                for h in range(MH):
                    last = STT(yT[:, h, :], b4(4)[:, h, :], gn_g[:, h:h + 1], skip_c[:, h, :], ALU.mult, ALU.add)
                last.then_inc(ym_ready, 1)

            Lz = Links(dve, dve_s, 1)

            def make_sp(T, i):
                c = units_before(T) + i
                Lz.at(c)
                for hg in range(2):
                    dve.wait_ge(ln_ready, 2 * c + hg + 1)
                    last = STT(sp_[hg], bank[2 + hg][:, :], 0.0, zl[hg], ALU.max, ALU.add)
                    if not diagonal(i):
                        last.then_inc(sp_ready, 1)
                if not diagonal(i):
                    dve.sem_inc(dve_s, 1)
                    Lz.k += 1
                    return
                Lz(last)
                for hg in range(2):
                    v = sp_[hg].rearrange("p (c t) -> p c t", c=SHP)
                    TT(v, v, before[:, :].unsqueeze(1).broadcast_to([P, SHP, P]), ALU.mult).then_inc(sp_ready, 1)

            def add_later(T, i):
                c = units_before(T) + i
                dve.wait_ge(s_done, 2 * c + 2)
                dve.wait_ge(sp_ready, 2 * c + 2)
                for hg in range(2):
                    if diagonal(i):
                        last = nc.vector.tensor_copy(later[hg], sp_[hg])
                    else:
                        last = TT(later[hg], later[hg], sp_[hg], ALU.add)
                last.then_inc(later_ready, 1)
                dve.wait_ge(later_ready, c + 1)

            def sum_o(T):
                dve.wait_ge(osq_ready, T)
                nc.vector.tensor_reduce(oss, osq.rearrange("p (h d) -> p h d", h=SH), AX_X, ALU.add).then_inc(
                    oss_ready, 1)

            def make_on(T):
                dve.wait_ge(ors_ready, T)
                TT(on.rearrange("p (h d) -> p h d", h=SH), bank[5][:, :].rearrange("p (h d) -> p h d", h=SH),
                   wide(ors, [P, SH, SD]), ALU.mult).then_inc(on_ready, 1)

            def make_h2(T):
                dve.wait_ge(mixed, T)
                dve.wait_ge(x_in, 16 * T)
                for i in range(2):
                    last = TT(hx[:, 512 * i:512 * i + 512], hx[:, 512 * i:512 * i + 512], bank[6 + i][:, :], ALU.add)
                last.then_inc(h_ready, 1)

            def make_n2(T):
                dve.wait_ge(hrs_ready, T)
                STT(n2_next[:, :], hx, hrs, g_ffn_b[:, :], ALU.mult, ALU.mult).then_inc(n2_ready, 1)

            Lt = Links(dve, dve_t, 12 * PH)

            def LT(ins):
                Lt(ins)
                dve.sem_inc(dve_turn, 1)

            def top16(values, indices, src, spare):
                nc_v = nc.vector
                LT(nc_v.max(values[:, 0:8], src))
                nc_v.max_index(indices[:, 0:8], values[:, 0:8], src)
                LT(nc_v.match_replace(spare, values[:, 0:8], src, LOWEST))
                LT(nc_v.max(values[:, 8:16], spare))
                return nc_v.max_index(indices[:, 8:16], values[:, 8:16], spare)

            def halves(h):
                def f(T):
                    if h == 0:
                        Lt.at(T - 1)
                    if h % 2 == 0:
                        dve.wait_ge(scores_done, 4 * (T - 1) + h // 2 + 1)
                        dve.sem_inc(dve_turn, 1)
                    for p in range(2):
                        src = b4(6 + h // 2 % 2)[:, 2 * (h % 2) + p, :]
                        last = top16(srt[:, p, :], sri[:, p, :], src, rest[:, p * NKEY:(p + 1) * NKEY])
                    LT(last)
                    if h % 2 == 1:
                        dve.sem_inc(scores_read, 1)
                return f

            def pair_sums(h):
                def f(T):
                    LT(TT(cand[:, :, :], wide(srt[:, 0, :], [P, TOPK, TOPK]),
                          srt[:, 1, :].unsqueeze(1).broadcast_to([P, TOPK, TOPK]), ALU.add))
                    LT(top16(best[:, h, :], pos[:, :], cand[:, :, :].rearrange("p a b -> p (a b)"), rest[:, :]))
                return f

            def choose(h):
                def f(T):
                    E = 6 * ((T - 1) * PH + h)
                    TSi(half[:, 0, :], pos[:, :], 4, ALU.logical_shift_right)
                    TSi(half[:, 1, :], pos[:, :], 15, ALU.bitwise_and).then_inc(dve_e, 1)
                    dve.wait_ge(dve_e, E + 1)
                    r2 = [rest[:, :].rearrange("p (k i) -> p k i", k=TOPK), cand[:, :, :]]
                    for q in range(2):
                        last = TT(r2[q], wide(half[:, q, :], [P, TOPK, TOPK]),
                                  iota16[:, :].unsqueeze(1).broadcast_to([P, TOPK, TOPK]), ALU.is_equal)
                    last.then_inc(dve_e, 1)
                    dve.wait_ge(dve_e, E + 2)
                    for q in range(2):
                        last = TT(r2[q], r2[q], sri[:, q, :].unsqueeze(1).broadcast_to([P, TOPK, TOPK]), ALU.mult)
                    last.then_inc(dve_e, 1)
                    dve.wait_ge(dve_e, E + 3)
                    for q in range(2):
                        last = nc.vector.tensor_reduce(sel[:, q, :], r2[q], AX_X, ALU.add)
                    last.then_inc(dve_e, 1)
                    dve.wait_ge(dve_e, E + 4)
                    STT(chosen[:, bass.ds((T - 1) * NJ + h * TOPK, TOPK)], sel[:, 0, :], float(NKEY), sel[:, 1, :],
                        ALU.mult, ALU.add).then_inc(idx_ready, 1)
                    dve.sem_inc(dve_e, 2)
                return f

            def TSi(out_, a, s, op):
                return nc.vector.tensor_scalar(out_, a, s, None, op)

            def soften(T):
                TT(gate_next[:, :, :], best[:, :, :], best[:, :, 0:1].broadcast_to([P, PH, TOPK]),
                   ALU.subtract).then_inc(soft_in, 1)

            Lg = Links(dve, dve_g, 3)

            def divide(T):
                dve.wait_ge(soft_exp, T)
                Lg.at(T - 1)
                Lg(nc.vector.tensor_reduce(gsum[:, 0, :], gate_next[:, :, :], AX_X, ALU.add))
                Lg(nc.vector.reciprocal(gsum[:, 1, :], gsum[:, 0, :]))
                Lg(TT(gate_next[:, :, :], gate_next[:, :, :], wide(gsum[:, 1, :], [P, PH, TOPK]), ALU.mult))

            hooks = {(0, 0): set_now, (0, 2): make_kw, (0, 5): make_p, (1, 0): make_h, (1, 2): make_hn,
                     (1, 3): make_ym, (1, 5): lambda T: make_sp(T, 0),
                     (1, 6): lambda T: add_later(T, 0),
                     (11, 1): sum_o, (11, 3): make_on, (12, 1): make_h2, (12, 3): make_n2}
            for h in range(PH):
                first = 12 * GROUP + 7 + 3 * h
                for n, f in enumerate((halves(h), pair_sums(h), choose(h))):
                    hooks[divmod(first + n, GROUP)] = f
            hooks[15, 7] = both_of(hooks[15, 7], soften) if (15, 7) in hooks else soften
            middle = {3: make_sp, 5: add_later}

            set_now(0)
            make_kw(0)
            update_state(0)
            in_order(1, hooks, middle)
            divide(1)

            def begin(T, dot, sums):
                if dot:
                    wait(dve, u_free, RING + (T - 1) * NJ)
                    dve.wait_ge(n2_ready, T)
                    dve.sem_inc(dve_turn, 1)
                    nc.vector.tensor_copy(xs[:, :], n2_next[:, :]).then_inc(xs_ready, 1)
                    nc.vector.tensor_copy(gate_now[:, :], gate_next[:, :, :].rearrange("p a b -> p (a b)")).then_inc(
                        xs_ready, 1)
                    dve.wait_ge(xs_ready, 2 * T)

            def group(T, g, at_pick, Tf, dot, sums):
                a = (T - 1) * GROUPS + g
                fixed = isinstance(g, int)
                for jj in range(GROUP):
                    if dot:
                        dve.wait_ge(u_landed[jj % RING], ((T - 1) * GROUPS + g) * (16 * GROUP // RING)
                                    + 16 * (jj // RING + 1))
                        s = ring_u[:, jj % RING, :]
                        col = dots[:, g * GROUP + jj:g * GROUP + jj + 1] if fixed else dots8[:, jj:jj + 1]
                        nc.vector.tensor_tensor_reduce(s, s, xs[:, :], 1.0, 0.0, ALU.mult, ALU.add,
                                                       col).then_inc(u_free, 1)
                    if jj in at_pick:
                        at_pick[jj](Tf)
                if dot and not fixed:
                    dve.wait_ge(u_free, RING + (a + 1) * GROUP)
                    dve.sem_inc(dve_turn, 1)
                    nc.vector.tensor_copy(dots[:, bass.ds(g * GROUP, GROUP)], dots8[:, :]).then_inc(dots_moved, 1)
                    dve.wait_ge(dots_moved, (T - 1) * MIDDLE + g - (PRE - 1))

            def end(T, dot, sums):
                if dot:
                    dve.wait_ge(gelu_ready, T)
                    TT(wgt[:, :], dots[:, :], gate_now[:, :], ALU.mult).then_inc(wgt_ready, 1)
                    dve.wait_ge(wgt_ready, T)
                    if not (isinstance(T, int) and T == LAST):
                        divide(T + 1)
                if sums:
                    dve.wait_ge(v_free, RING + (T - 1) * NJ)
                    dve.wait_ge(res_in, 16 * (T - 1))
                    TT(y_res[:, :], acc[:, :, :].rearrange("p a b -> p (a b)"), y_res[:, :], ALU.add).then_inc(
                        acc_read, 1)
                    dve.wait_ge(yrs_ready, T - 1)
                    dve.wait_ge(acc_read, T - 1)
                    STT(y_res[:, :], y_res[:, :], yrs, g_fin_b[:, :], ALU.mult, ALU.mult).then_inc(y_ready, 1)

            dve.sem_inc(u_free, RING)
            expert_steps(dve, group, end, begin, hooks, middle)

        @block.tensor
        def _(pe):
            def mm(out_, lhsT, rhs, start=True, stop=True):
                return nc.tensor.matmul(out_, lhsT, rhs, start=start, stop=stop, skip_group_check=True)

            pe.wait_ge(fills, FILLS)

            def square_sums(T):
                pe.wait_ge(squared, T + 1)
                wait(pe, rs_ready, T)
                for k in range(KC):
                    last = mm(sum_psum, ones[:, :], sqT[:, k, :], k == 0, k == KC - 1)
                last.then_inc(summed, 1)

            def tile_step(T, p, k):
                lead = isinstance(T, int) and T == 0
                pe.wait_ge(n_ready, T + 1)
                for n, a, w in COLS:
                    if lead and n in ("qs", "so"):
                        continue
                    t = T - 1 if n in ("qs", "so") else T
                    pe.wait_ge(w_landed[n], 16)
                    wait(pe, unit_taken[n], t)
                    if n in ("u", "ks", "qs"):
                        for c in range(4):
                            for kk in range(KC):
                                last = mm(b4(PSUM_OF[n])[:, c, :], w_in_sb[:, kk, a + c * P:a + (c + 1) * P],
                                          nT[p][:, kk, :], kk == 0, kk == KC - 1)
                    else:
                        dst = gate_psum if n == "gates" else bank[PSUM_OF[n]][:, :]
                        for kk in range(KC):
                            last = mm(dst, nT[p][:, kk, :], w_in_sb[:, kk, a:a + w], kk == 0, kk == KC - 1)
                    last.then_inc(unit_done[n], 1)
                    if n == "u" and not (isinstance(T, int) and T == LAST):
                        square_sums(T + 1)

            square_sums(0)
            project(pe, tile_step)

            pe.wait_ge(gate_in, 1)
            pe.wait_ge(unit_taken["u"], TILES)
            mm(bank[2][:, 0:W36], tri[:, :], lf).then_inc(gate_pe, 1)
            pe.wait_ge(gate_in, 2)
            pe.wait_ge(unit_taken["qs"], LAST)
            pe.wait_ge(unit_taken["so"], LAST)
            pe.wait_ge(unit_taken["vs"], TILES)
            for T in range(TILES):
                mm(bank[3 + T // 4][0:MH, T % 4 * P:(T % 4 + 1) * P], cols[:, 0, T * MH:(T + 1) * MH], ident[:, :])
            for T in range(TILES):
                last = mm(bank[(6, 7, 2)[T // 4]][0:MH, T % 4 * P:(T % 4 + 1) * P], tmp36[:, T * MH:(T + 1) * MH],
                          ident[:, :])
            last.then_inc(gate_pe, 1)
            pe.wait_ge(gate_in, 3)
            for n, rows in enumerate((rows_wi, rows_em, rows_ws)):
                for T in range(TILES):
                    mm(bank[3][:, n * W36 + T * MH:n * W36 + (T + 1) * MH], rows[:, T * P:(T + 1) * P],
                       ident[0:MH, 0:MH])
            mm(bank[4][:, 0:W36], ones[0:MH, :], dec_blk).then_inc(gate_pe, 1)

            def qk(T):
                lead = isinstance(T, int) and T == 0
                pe.wait_ge(mix_in, 32 + 64 * T)
                if lead:
                    pe.wait_ge(gates_ready, 1)
                elif not (isinstance(T, int) and T == 1):
                    pe.wait_ge(idx_ready, (T - 1) * PH)
                if not lead:
                    for h in range(MH):
                        mm(b4(2)[:, h, :], w_qk[:, 0, h, :], cT[:, h, :])
                    for h in range(MH):
                        mm(b4(3)[:, h, :], w_qk[:, 1, h, :], cT[:, h, :])
                for h in range(MH):
                    last = mm(b4(4)[:, h, :], cT[:, h, :], w_qk[:, 1, h, :])
                last.then_inc(qk_done, 1)

            def se(T):
                pe.wait_ge(qk_copied, T)
                pe.wait_ge(m_blk_ready, T)
                for h in range(MH):
                    mm(b4(2)[:, h, :], k_m[:, h, :], q_m[:, h, :])
                mm(bank[3][:, :], ones[0:MH, :], m_blk[:, :, :].rearrange("p h t -> p (h t)"), True, False)
                mm(bank[3][:, :], ident_h[:, :], neg_m[:, :].unsqueeze(1).broadcast_to([P, MH, P]), False,
                   True).then_inc(se_done, 1)

            def hh(T):
                pe.wait_ge(p_ready, T)
                pe.wait_ge(kw_ready, T + 1)
                pe.wait_ge(state_ready, T)
                for h in range(MH):
                    mm(b2(4 + h // 2)[:, h % 2, :], wexp[:, h, :], vx[:, h, :])
                for h in range(MH):
                    last = mm(b2(6 + h // 2)[:, h % 2, :], q_m[:, h, :], state[:, h, :])
                last.then_inc(hh_done, 1)
                dstate(T)

            def dstate(T):
                for h in range(MH):
                    last = mm(b2(2 + h // 2)[:, h % 2, :], kw[:, h, :], vx[:, h, :])
                last.then_inc(dstate_done, 1)

            def hn_t(T):
                pe.wait_ge(hn_ready, T)
                for h in range(MH):
                    last = nc.tensor.transpose(b4(4)[:, h, :], hb[:, h, :], ident[:, :])
                last.then_inc(hnT_done, 1)

            def z(T, i):
                c = units_before(T) + i
                pe.wait_ge(k_in, 16 * (c + 1))
                if diagonal(i):
                    pe.wait_ge(state_ready, T + 1)
                    pe.wait_ge(mix_in, 32 + 64 * T)
                wait(pe, a_ready, 2 * c)
                for hg in range(2):
                    r = slice(SD * hg, SD * hg + SD)
                    for cc in range(SHP):
                        last = mm(bank[2 + hg][:, cc * P:(cc + 1) * P], keys[r, cc, :], qsT[r, cc, :], cc == 0,
                                  False)
                    last.then_inc(z_done, 1)

            def s(T, i):
                c = units_before(T) + i
                for hg in range(2):
                    pe.wait_ge(sp_ready, 2 * c + hg + 1)
                    b = bank[2 + hg][:, :]
                    last = mm(b, neg_tri[:, :], sp_[hg], False, False)
                    if diagonal(i):
                        last = mm(b, ident_h[:, :], neg_s[:, :].unsqueeze(1).broadcast_to([P, SHP, P]), False, True)
                    else:
                        if hg == 0:
                            pe.wait_ge(later_ready, c)
                        last = mm(b, neg_ones[:, :], later[hg], False, True)
                    last.then_inc(s_done, 1)

            def av(T, i):
                c = units_before(T) + i
                pe.wait_ge(v_in, 16 * (c + 1))
                for hg in range(2):
                    pe.wait_ge(a_ready, 2 * c + hg + 1)
                    for cc in range(SHP):
                        h = 2 * cc + hg
                        last = mm(bank[5][:, h * SD:(h + 1) * SD], zl[hg][:, cc * P:(cc + 1) * P], vals[:, h, :],
                                  diagonal(i) and h == 0, True)
                last.then_inc(av_done, 1)

            def on_t(T):
                pe.wait_ge(on_ready, T)
                for c in range(4):
                    last = nc.tensor.transpose(b4(2)[:, c, :], on[:, c * P:(c + 1) * P], ident[:, :])
                last.then_inc(onT_done, 1)

            def w_out_part(i):
                def f(T):
                    if i == 0:
                        pe.wait_ge(ym_ready, T)
                        pe.wait_ge(ys_ready, T)
                        pe.wait_ge(w2_landed, 32)
                    n, k0 = i // 2, i % 2 * 4
                    for k in range(k0, k0 + 4):
                        last = mm(bank[6 + n][:, :], yT[:, k, :], w_out_sb[:, k, n * 512:(n + 1) * 512], k == 0,
                                  k == KC - 1)
                    if i == 3:
                        last.then_inc(mixed, 1)
                return f

            def n2_t(T):
                pe.wait_ge(n2_ready, T)
                for k in range(KC):
                    last = nc.tensor.transpose(b4(2 + k // 4)[:, k % 4, :], n2_next[:, k * P:(k + 1) * P],
                                               ident[:, :])
                last.then_inc(n2T_done, 1)

            def query(q4, c0, c1):
                def f(T):
                    if c0 == 0:
                        pe.wait_ge(n2T_copied, T)
                        if q4 >= 2:
                            pe.wait_ge(qp_copied, 4 * (T - 1) + q4 - 1)
                    for c in range(c0, c1):
                        a = (4 * q4 + c) * P
                        for k in range(KC):
                            last = mm(b4(4 + q4 % 2)[:, c, :], w_q_sb[:, k, a:a + P], n2T[:, k, :], k == 0,
                                      k == KC - 1)
                    if c1 == 4:
                        last.then_inc(qp_done, 1)
                return f

            def scores(q4):
                def f(T):
                    pe.wait_ge(qp_copied, 4 * (T - 1) + q4 + 1)
                    if q4 >= 2:
                        pe.wait_ge(scores_read, 4 * (T - 1) + q4 - 1)
                    else:
                        pe.wait_ge(h_ready, T)
                    for c in range(4):
                        last = mm(b4(6 + q4 % 2)[:, c, :], qp[q4 % 2][:, c, :], subT[:, c % 2, :])
                    last.then_inc(scores_done, 1)
                return f

            hooks = {(0, 0): qk, (0, 3): se, (0, 6): hh, (1, 2): hn_t, (1, 4): lambda T: z(T, 0),
                     (1, 6): lambda T: s(T, 0), (1, 7): lambda T: av(T, 0), (11, 3): on_t,
                     (11, 5): w_out_part(0), (11, 6): w_out_part(1), (11, 7): w_out_part(2), (12, 0): w_out_part(3),
                     (12, 4): n2_t, (12, 5): query(0, 0, 4), (12, 6): scores(0),
                     (12, 7): query(1, 0, 2), (13, 0): query(1, 2, 4), (13, 2): scores(1),
                     (13, 4): query(2, 0, 2), (13, 6): query(2, 2, 4), (14, 1): scores(2),
                     (14, 2): query(3, 0, 2), (14, 4): query(3, 2, 4), (14, 7): scores(3)}
            middle = {0: z, 3: s, 6: av}

            qk(0)
            pe.wait_ge(kw_ready, 1)
            dstate(0)
            in_order(1, hooks, middle)

            def begin(T, dot, sums):
                if sums:
                    wait(pe, acc_read, T - 2)

            def group(T, g, at_pick, Tf, dot, sums):
                b = (T - 2) * GROUPS + g
                for jj in range(GROUP):
                    if sums:
                        pe.wait_ge(diag_ready, b * GROUP + jj + 1)
                        pe.wait_ge(v_landed[jj % RING], b * (16 * GROUP // RING) + 16 * (jj // RING + 1))
                        first = isinstance(g, int) and g == 0 and jj == 0
                        final = isinstance(g, int) and g == GROUPS - 1 and jj == GROUP - 1
                        for n in range(2):
                            last = mm(acc[:, n, :], diag[:, jj % 4, :], ring_v[:, jj % RING, n * 512:(n + 1) * 512],
                                      first, final)
                        last.then_inc(v_free, 1)
                    if jj in at_pick:
                        at_pick[jj](Tf)

            pe.sem_inc(v_free, RING)
            expert_steps(pe, group, lambda T, dot, sums: None, begin, hooks, middle)


_ARGS = ["xT", "xn_in", "w_in", "w_out", "w_query", "sub_t", "mlstm_w", "gain_cols", "g_ffn", "g_final",
         "gate_bias", "expert_u", "expert_v"]


def kernel(x, meta, norm_mix_g, w_in, conv_w, conv_b, w_qm, w_km, b_i, b_f, mlstm_skip, mlstm_gn_g,
           sb_norm_g, w_out, norm_ffn_g, w_query, sub_keys, expert_u, expert_v, norm_final_g):
    import numpy as np
    import concourse.bacc as bacc
    from concourse.bass_utils import run_bass_kernel_spmd

    def cols(a):
        return np.asarray(a).reshape(-1, P).T

    x, meta = np.asarray(x), np.asarray(meta)
    rows = np.concatenate([np.zeros((P - N_META, D), x.dtype), meta, x[0]], axis=0)
    taps = np.asarray(conv_w)[0].reshape(CONV, MH, P).transpose(2, 1, 0).reshape(P, MH * CONV)
    arrays = {
        "xT": rows.T,
        "xn_in": rows,
        "w_in": np.asarray(w_in)[0],
        "w_out": np.asarray(w_out)[0],
        "w_query": np.asarray(w_query)[0],
        "sub_t": np.asarray(sub_keys)[0].transpose(2, 0, 1),
        "mlstm_w": np.stack([np.asarray(w_qm)[0], np.asarray(w_km)[0]]).transpose(2, 0, 1, 3),
        "gain_cols": np.concatenate([cols(norm_mix_g), cols(mlstm_gn_g), cols(mlstm_skip), cols(sb_norm_g), taps,
                                     cols(conv_b)], axis=1),
        "g_ffn": np.asarray(norm_ffn_g),
        "g_final": np.asarray(norm_final_g)[None],
        "gate_bias": np.concatenate([np.asarray(b_i), np.asarray(b_f)], axis=1),
        "expert_u": np.asarray(expert_u)[0],
        "expert_v": np.asarray(expert_v)[0],
    }
    nc = bacc.Bacc("TRN2", target_bir_lowering=False, num_devices=1)
    arrays = {n: np.ascontiguousarray(a) for n, a in arrays.items()}
    args = [nc.dram_tensor(n, arrays[n].shape, F32, kind="ExternalInput").ap() for n in _ARGS]
    args.append(nc.dram_tensor("out", (SEQ, D), F32, kind="ExternalOutput").ap())
    program(nc, *args)
    r = run_bass_kernel_spmd(nc, [arrays], core_ids=[0])
    return r.results[0]["out"].reshape(1, SEQ, D)
```

```python
from contextlib import ExitStack

import concourse.bass as bass
from concourse import mybir

F32 = mybir.dt.float32
BF16 = mybir.dt.bfloat16
I32 = mybir.dt.int32
U32 = mybir.dt.uint32
ALU = mybir.AluOpType
ACT = mybir.ActivationFunctionType
AX_X = mybir.AxisListType.X

P = 128
D = 1024
KC = D // P
SEQ = 1024
N_META = 16
TILES = (P + SEQ) // P
LAST = TILES - 1
MH, MD = 4, 128
SH, SD = 8, 64
SHP = SH // 2
MIX = MH * MD
CONV = 4
D_IN = 6 * MIX + 2 * MH
PH, TOPK, NKEY = 8, 16, 128
NJ = PH * TOPK
EPS = 1e-6
NEG = -1e30
LOWEST = -3.4e38

GROUP = 8
GROUPS = NJ // GROUP
RING_U, RING_V = 4, 8
PRE = 3
MIDDLE = PH
N2_MOVES = (13, 6)
FILLS = 11
N_CONSTS, N_LATE = 2, 2


def units_before(T):
    return (T * T + T - 2) // 2


def wait(eng, sem, value):
    if isinstance(value, int) and value <= 0:
        return
    eng.wait_ge(sem, value)


def diagonal(i):
    return isinstance(i, int) and i == 0


class Links:

    def __init__(self, eng, sem, per):
        self.eng, self.sem, self.per, self.base, self.k = eng, sem, per, 0, per

    def at(self, turn):
        assert self.k == self.per, (self.k, self.per)
        self.base, self.k = turn * self.per, 0

    def __call__(self, ins):
        self.k += 1
        ins.then_inc(self.sem, 1)
        self.eng.wait_ge(self.sem, self.base + self.k)


def program(nc, xT, xn_in, w_in, w_out, w_queryT, sub_t, mlstm_w, gain_cols, g_final,
            gate_bias, expert_u, expert_v, out):
    with ExitStack() as ctx:
        def sb(name, shape, dt=F32):
            return ctx.enter_context(nc.sbuf_tensor(name, shape, dt))

        def sem(name):
            return ctx.enter_context(nc.semaphore(name))

        mix_dram = nc.dram_tensor("mix_dram", (TILES, P, 4 * MIX), F32).ap()
        kv_dram = nc.dram_tensor("kv_dram", (TILES, P, 2 * MIX), F32).ap()
        top_dram = nc.dram_tensor("top_dram", (MH, TILES * P), F32).ap()
        res_dram = nc.dram_tensor("res_dram", (TILES, P, D), F32).ap()

        weights = sb("weights", [P, KC * D_IN])
        w_in_sb = weights[:, :].rearrange("p (k n) -> p k n", k=KC)
        w_out_sb = weights[:, 0:KC * D].rearrange("p (k n) -> p k n", k=KC)
        w_qT = weights[:, KC * D:3 * KC * D].rearrange("p (j k) -> p j k", j=2 * PH)
        w_score = weights[:, KC * D:3 * KC * D].rearrange("p (j k n) -> p j k n", j=2 * PH, k=KC)

        sizes = {}
        top = 0
        for name, n in (("ring_u", RING_U * D), ("ring_v", RING_V * D), ("arena", 3080), ("keys", MIX),
                        ("vals", MIX), ("cso", 3 * MIX), ("vx", MH * (MD + 1))):
            sizes[name] = (top, top + n)
            top += n
        work = sb("work", [P, top])

        def part(name):
            a, b = sizes[name]
            return work[:, a:b]

        ring_u = part("ring_u").rearrange("p (s d) -> p s d", s=RING_U)
        ring_v = part("ring_v").rearrange("p (s d) -> p s d", s=RING_V)
        arena = part("arena")
        keys = part("keys").rearrange("p (c s) -> p c s", c=SHP)
        vals = part("vals").rearrange("p (h d) -> p h d", h=SH)
        cso = part("cso").rearrange("p (a n) -> p a n", a=3)
        cT = cso[:, 0, :].rearrange("p (h t) -> p h t", h=MH)
        so = cso[:, 1, :].rearrange("p (h e) -> p h e", h=MH)
        yT = cso[:, 0:2, :].rearrange("p a (h t) -> p (a h) t", h=MH)
        qsT = cso[:, 2, :].rearrange("p (c t) -> p c t", c=SHP)
        vx = part("vx").rearrange("p (h e) -> p h e", h=MH)

        cut = [0]

        def take(n):
            a = cut[0]
            cut[0] += n
            return work[:, a:a + n]

        xT_sb = [take(D).rearrange("p (k t) -> p k t", k=KC) for _ in range(2)]
        nT = [take(D).rearrange("p (k t) -> p k t", k=KC) for _ in range(2)]
        sqT = take(D).rearrange("p (k t) -> p k t", k=KC)
        stage = [take(6 * MIX) for _ in range(2)]
        ucat = take(MH * (P + 3)).rearrange("p (h t) -> p h t", h=MH)
        conv = take(MIX).rearrange("p (h t) -> p h t", h=MH)
        sig = take(MIX).rearrange("p (h t) -> p h t", h=MH)
        rsT = [take(P) for _ in range(2)]
        tri = work[:, top - P:]
        assert cut[0] <= top - P
        cut[0] = 0
        W36 = TILES * MH
        lf = take(W36)
        tmp36 = take(W36)
        li = take(W36)
        rows_a = take(TILES * P)[0:MH, :]
        rows_b = take(TILES * P)[0:MH, :]
        rows_M = take(TILES * P)[0:MH, :]
        rows_wi = take(TILES * P)[0:MH, :]
        rows_em = take(TILES * P)[0:MH, :]
        rows_ws = take(TILES * P)[0:MH, :]
        m_row = take(TILES + 1)[0:MH, :]
        dec_row = take(TILES)[0:MH, :]
        dec_blk = take(W36)[0:MH, :]

        def at(a, n):
            return arena[:, a:a + n]

        q_m = at(0, 512).rearrange("p (h t) -> p h t", h=MH)
        k_m = at(512, 512).rearrange("p (h t) -> p h t", h=MH)
        kw = at(1024, 512).rearrange("p (h e) -> p h e", h=MH)
        wexp = at(1536, 512).rearrange("p (h t) -> p h t", h=MH)
        inter = at(2048, 516).rearrange("p (h e) -> p h e", h=MH)
        nd = at(2564, 516).rearrange("p (h e) -> p h e", h=MH)
        m_blk = at(2564, 512)[0:MH, :].rearrange("p (h t) -> p h t", h=MH)
        skip_c = q_m
        hb = k_m
        hsq = at(2048, 512).rearrange("p (h e) -> p h e", h=MH)
        zl = [at(512 * i, 512) for i in range(2)]
        sp_ = [at(1024 + 512 * i, 512) for i in range(2)]
        later = [at(2048 + 512 * i, 512) for i in range(2)]
        osq = at(0, 512)
        on = at(512, 512)
        square_out = at(0, 1024)
        y_res = at(1024, 1024)
        g_fin = at(0, 1024)
        hx = at(2048, 1024)

        n2_next = sb("n2_next", [P, D])
        xs = sb("xs", [P, D])
        n2T = sb("n2T", [P, KC, P])
        w_qk = sb("w_qk", [P, 2, MH, MD])
        state = sb("state", [P, MH, MD + 1])
        chosen, chosen_u, chosen_v = (sb(n, [P, NJ], I32) for n in ("chosen", "chosen_u", "chosen_v"))
        idx_u = [sb(f"idx_u{i}", [P, GROUP], I32) for i in range(2)]
        idx_v = [sb(f"idx_v{i}", [P, GROUP], I32) for i in range(2)]
        gate_next = sb("gate_next", [P, PH, TOPK])
        gate_now = sb("gate_now", [P, NJ])
        dots = sb("dots", [P, NJ])
        dots8 = sb("dots8", [P, GROUP])
        wgt = sb("wgt", [P, NJ])
        wgt8 = sb("wgt8", [P, GROUP])
        diag = sb("diag", [P, 4, P])
        ident = sb("ident", [P, P])
        ident_h = sb("ident_h", [P, P], BF16)
        neg_m = sb("neg_m", [P, P], BF16)
        neg_s = sb("neg_s", [P, P], BF16)
        before = sb("before", [P, P])
        neg_tri = sb("neg_tri", [P, P])
        ones = sb("ones", [P, P])
        subT = sb("subT", [P, 2, NKEY])
        m_top = sb("m_top", [MH, P])
        neg_blk = sb("neg_blk", [MH, MH, P])
        cols = sb("cols", [P, 5, W36])
        now = sb("now", [P, 5, MH])
        graw = sb("graw", [P, TILES, 2 * MH])
        gains = sb("gains", [P, KC + 3 * MH + MH * CONV + MH + KC])
        g_mix = gains[:, 0:8]
        gn_g = gains[:, 8:12]
        skip_g = gains[:, 12:16]
        sb_g = gains[:, 16:20]
        conv_w = gains[:, 20:36]
        conv_b = gains[:, 36:40]
        g_ffn = gains[:, 40:48]
        gbias = sb("gbias", [P, 2 * MH])
        eps = sb("eps", [P, 1])
        one = sb("one", [P, 1])
        valid = sb("valid", [P, 1])
        invalid = sb("invalid", [P, 1])
        small = sb("small", [P, 48])
        den, mean, var, rstd = (small[:, 4 * i:4 * i + 4] for i in range(4))
        oss, ors = small[:, 16:24], small[:, 24:32]
        hss, hrs, yss, yrs = (small[:, 32 + i:33 + i] for i in range(4))
        srt = sb("srt", [P, 2, TOPK])
        sri = sb("sri", [P, 2, TOPK], U32)
        rest = sb("rest", [P, 256])
        cand = sb("cand", [P, TOPK, TOPK])
        best = sb("best", [P, PH, TOPK])
        best_h = sb("best_h", [P, TOPK])
        pos = sb("pos", [P, TOPK], U32)
        half = sb("half", [P, 2, TOPK], U32)
        iota16 = sb("iota16", [P, TOPK])
        iota_i = sb("iota_i", [P, TOPK], I32)
        sel = sb("sel", [P, 2, TOPK])
        gsum = sb("gsum", [P, 2, PH])

        acc = ctx.enter_context(nc.psum_tensor("acc", [P, 2, 512], F32))
        bank = [None, None] + [ctx.enter_context(nc.psum_tensor(f"bank{i}", [P, 512], F32)) for i in range(2, 8)]

        def b4(i):
            return bank[i][:, :].rearrange("p (h t) -> p h t", h=4)

        def b2(i):
            return bank[i][:, 0:2 * (MD + 1)].rearrange("p (h e) -> p h e", h=2)

        consts_in, late_in, g_fin_in = sem("consts_in"), sem("late_in"), sem("g_fin_in")
        fill = sem("fill")
        fills = sem("fills")
        COLS = [("u", 0, MIX), ("ks", 2056, MIX), ("qs", 1544, MIX), ("v", 512, MIX),
                ("so", 1024, MIX), ("vs", 2568, MIX), ("gates", 1536, 2 * MH)]
        w_landed = {n: sem(f"w_landed_{n}") for n, _, _ in COLS}
        x_landed = [sem(f"x_landed{i}") for i in range(2)]
        squared, summed, rs_ready, n_ready = sem("squared"), sem("summed"), sem("rs_ready"), sem("n_ready")
        unit_done = {n: sem(f"{n}_done") for n, _, _ in COLS}
        unit_taken = {n: sem(f"{n}_taken") for n, _, _ in COLS}
        conv_ready, conv_exp, hist_moved = sem("conv_ready"), sem("conv_exp"), sem("hist_moved")
        staged_act, staged_dve = sem("staged_act"), sem("staged_dve")
        stored = [sem(f"stored{i}") for i in range(2)]
        act_p, dve_p = sem("act_p"), sem("dve_p")
        gate_in, gate_pe, gate_act, gate_dve, rows_ready, top_ready, top_stored, gates_ready = (
            sem("gate_in"), sem("gate_pe"), sem("gate_act"), sem("gate_dve"), sem("rows_ready"), sem("top_ready"),
            sem("top_stored"), sem("gates_ready"))
        w_out_landed = sem("w_out_landed")
        w_q_landed = [sem(f"w_q_landed{i}") for i in range(4)]
        fold_done, fold_copied = sem("fold_done"), sem("fold_copied")
        mix_in = sem("mix_in")
        now_ready, m_blk_ready = sem("now_ready"), sem("m_blk_ready")
        qk_done, qk_copied, kw_ready = sem("qk_done"), sem("qk_copied"), sem("kw_ready")
        se_done, wexp_ready, p_ready = sem("se_done"), sem("wexp_ready"), sem("p_ready")
        hh_done, dstate_done, inter_ready, state_ready = (
            sem("hh_done"), sem("dstate_done"), sem("inter_ready"), sem("state_ready"))
        var_ready, rstd_ready, hn_ready, hnT_done, skip_ready, ym_ready = (
            sem("var_ready"), sem("rstd_ready"), sem("hn_ready"), sem("hnT_done"), sem("skip_ready"), sem("ym_ready"))
        k_in, v_in = sem("k_in"), sem("v_in")
        z_done, ln_ready, sp_ready, s_done, later_ready, a_ready, av_done = (
            sem("z_done"), sem("ln_ready"), sem("sp_ready"), sem("s_done"),
            sem("later_ready"), sem("a_ready"), sem("av_done"))
        osq_ready, oss_ready, ors_ready, on_ready, onT_done, ys_ready = (
            sem("osq_ready"), sem("oss_ready"), sem("ors_ready"), sem("on_ready"), sem("onT_done"), sem("ys_ready"))
        x_in, mixed, h_ready, h_stored, hrs_ready, n2_ready, n2T_done, n2T_copied, n2_back, n2_moved = (
            sem("x_in"), sem("mixed"), sem("h_ready"), sem("h_stored"), sem("hrs_ready"), sem("n2_ready"),
            sem("n2T_done"), sem("n2T_copied"), sem("n2_back"), sem("n2_moved"))
        scores_done, idx_ready, soft_in, soft_exp = (
            sem("scores_done"), sem("idx_ready"), sem("soft_in"), sem("soft_exp"))
        scores_free = sem("scores_free")
        dve_m, dve_s, dve_t, dve_e, dve_g = sem("dve_m"), sem("dve_s"), sem("dve_t"), sem("dve_e"), sem("dve_g")
        act_f, act_s, act_o, act_h, act_y = sem("act_f"), sem("act_s"), sem("act_o"), sem("act_h"), sem("act_y")
        dve_turn, act_turn, pool_turn, sp_turn = sem("dve_turn"), sem("act_turn"), sem("pool_turn"), sem("sp_turn")
        u_landed = [sem(f"u_landed{i}") for i in range(RING_U)]
        v_landed = [sem(f"v_landed{i}") for i in range(RING_V)]
        u_free, v_free = sem("u_free"), sem("v_free")
        chosen_moved = sem("chosen_moved")
        diag_ready, idx_u_copied, idx_v_copied = sem("diag_ready"), sem("idx_u_copied"), sem("idx_v_copied")
        xs_ready = sem("xs_ready")
        dots_moved, wgt_moved = sem("dots_moved"), sem("wgt_moved")
        gelu_ready, wgt_ready = sem("gelu_ready"), sem("wgt_ready")
        res_in, acc_read, yrs_ready, y_ready, out_stored = (
            sem("res_in"), sem("acc_read"), sem("yrs_ready"), sem("y_ready"), sem("out_stored"))

        block = ctx.enter_context(nc.Block())

        PSUM_OF = {"u": 2, "ks": 3, "qs": 4, "v": 5, "so": 6, "vs": 7}
        gate_psum = acc[:, 0, 0:2 * MH]
        sum_psum = acc[:, 1, 0:P]
        SLOT = {"c": 0, "v": 1, "so": 2, "qs": 3, "ks": 4, "vs": 5}

        def slot(p, name):
            return stage[p][:, SLOT[name] * MIX:(SLOT[name] + 1) * MIX]

        def slot4(p, name):
            return slot(p, name).rearrange("p (h t) -> p h t", h=4)

        def project(eng, tile_step):
            tile_step(0, 0, 0)
            tile_step(1, 1, 0)
            with eng.Fori(1, (TILES - 1) // 2) as k:
                tile_step(2 * k, 0, k)
                tile_step(2 * k + 1, 1, k)
            tile_step(LAST, 0, LAST // 2)

        def tile_of(dram, T):
            return dram[bass.ds(T, 1)].rearrange("a p n -> (a p) n")

        def wide(ap, shape):
            return ap.unsqueeze(len(shape) - 1).broadcast_to(shape)

        @block.sync
        def _(sp):
            def load_x(T, p):
                sp.dma_start(xT_sb[p], xT[:, bass.ds(T * P, P)].rearrange("(k p) t -> p k t", p=P)).then_inc(
                    x_landed[p], 16)

            load_x(0, 0)
            sp.dma_start(gains[:, :], gain_cols).then_inc(consts_in, 16)
            for n, a, w in COLS:
                sp.dma_start(w_in_sb[:, :, a:a + w],
                             w_in.rearrange("(k p) n -> p k n", p=P)[:, :, a:a + w]).then_inc(w_landed[n], 16)
                if n == "u":
                    sp.dma_start(gbias[:, :], gate_bias.broadcast_to([P, 2 * MH])).then_inc(consts_in, 16)
                    load_x(1, 1)
            sp.dma_start(w_qk[:, :, :, :], mlstm_w).then_inc(late_in, 16)
            sp.dma_start(subT[:, :, :], sub_t).then_inc(late_in, 16)

            def store(T, p, more=True):
                if more:
                    sp.wait_ge(n_ready, T + 1)
                    sp.wait_ge(squared, T + 1)
                    load_x(T + 2, p)
                sp.wait_ge(staged_act, T + 1)
                sp.wait_ge(staged_dve, T + 1)
                first = isinstance(T, int) and T == 0
                n = 2 * MIX if first else 4 * MIX
                sp.dma_start(tile_of(mix_dram, T)[:, 0:n], stage[p][:, 0:n]).then_inc(stored[p], 16)
                sp.dma_start(tile_of(kv_dram, T), stage[p][:, 4 * MIX:6 * MIX]).then_inc(stored[p], 16)

            store(0, 0)
            store(1, 1)
            with sp.Fori(1, 3) as k:
                store(2 * k, 0)
                store(2 * k + 1, 1)
            store(6, 0)
            store(7, 1, more=False)
            store(8, 0, more=False)
            sp.wait_ge(unit_done["gates"], TILES)
            for i in range(4):
                n = 2 * PH // 4
                sp.dma_start(w_qT[:, i * n:(i + 1) * n, :],
                             w_queryT.rearrange("(j c) k -> c j k", c=P)[:, i * n:(i + 1) * n, :]).then_inc(
                                 w_q_landed[i], 16)
            sp.dma_start(w_out_sb, w_out.rearrange("(k p) n -> p k n", p=P)).then_inc(w_out_landed, 16)
            sp.wait_ge(top_ready, 1)
            sp.dma_start(top_dram, rows_M).then_inc(top_stored, 16)
            sp.wait_ge(top_stored, 16)
            sp.wait_ge(stored[0], 32 * 5)
            sp.wait_ge(stored[1], 32 * 4)
            sp.wait_ge(gates_ready, 1)

            def load_mix(T):
                src = tile_of(mix_dram, T)
                lead = isinstance(T, int) and T == 0
                wait(sp, state_ready, T)
                if not lead:
                    wait(sp, ym_ready, T - 1)
                    wait(sp, av_done, units_before(T))
                sp.dma_start(cso[:, 0, :], src[:, 0:MIX]).then_inc(mix_in, 16)
                sp.dma_start(vx[:, :, 0:MD], src[:, MIX:2 * MIX].rearrange("p (h e) -> p h e", h=MH)).then_inc(
                    mix_in, 16)
                if lead:
                    return
                sp.dma_start(cso[:, 1:3, :], src[:, 2 * MIX:4 * MIX].rearrange("p (a n) -> p a n", a=2)).then_inc(
                    mix_in, 16)
                sp.dma_start(m_top[:, :], top_dram[:, bass.ds(T * P, P)]).then_inc(mix_in, 16)

            def load_kv(T, i):
                c = units_before(T) + i
                kb = T - i
                if not isinstance(kb, int):
                    kb = nc.s_assert_within(kb, 0, LAST, skip_runtime_bounds_check_because="i goes from 1 to T")
                src = tile_of(kv_dram, kb)
                wait(sp, z_done, 2 * c)
                sp.sem_inc(sp_turn, 1)
                sp.dma_start(keys, src[:, 0:MIX].rearrange("p (c s) -> p c s", c=SHP)).then_inc(k_in, 16)
                wait(sp, av_done, c)
                sp.dma_start(vals, src[:, MIX:2 * MIX].rearrange("p (h d) -> p h d", h=SH)).then_inc(v_in, 16)

            def load_res(T):
                sp.wait_ge(av_done, units_before(T + 1))
                sp.wait_ge(later_ready, units_before(T + 1))
                sp.dma_start(hx, xn_in[bass.ds(T * P, P), :]).then_inc(x_in, 16)
                sp.wait_ge(h_ready, T)
                sp.dma_start(tile_of(res_dram, T), hx).then_inc(h_stored, 16)

            def mix_loads(M):
                with sp.Fori(1, M + 1) as i:
                    load_kv(M, i)
                load_res(M)
                if not (isinstance(M, int) and M == LAST):
                    load_mix(M + 1)
                    load_kv(M + 1, 0)

            load_mix(0)
            load_mix(1)
            load_kv(1, 0)
            mix_loads(1)

            def step(T, mix=True, sums=True):
                if mix:
                    mix_loads(T + 2)
                if mix and sums:
                    sp.wait_ge(hrs_ready, T + 2)
                    sp.wait_ge(onT_done, T + 2)
                    sp.dma_start(g_fin, g_final.broadcast_to([P, D])).then_inc(g_fin_in, 16)
                if sums:
                    wait(sp, out_stored, 16 * (T - 2))
                    sp.wait_ge(h_stored, 16 * (T - 1))
                    sp.dma_start(y_res, tile_of(res_dram, T - 1)).then_inc(res_in, 16)
                    sp.wait_ge(y_ready, T - 1)
                    sp.dma_start(out[bass.ds((T - 2) * P, P), :], y_res).then_inc(out_stored, 16)

            step(0, sums=False)
            step(1, sums=False)
            step(2)
            with sp.Fori(3, LAST - 2) as T:
                step(T)
            step(LAST - 2)
            step(LAST - 1, mix=False)
            step(LAST, mix=False)
            step(LAST + 1, mix=False)
            sp.wait_ge(out_stored, 16 * LAST)
            sp.wait_ge(h_stored, 16 * LAST)

        @block.gpsimd
        def _(pool):
            def select(tile, sign, op, fill_value):
                pool.affine_select(out=tile[:, :], in_=tile[:, :], compare_op=op, fill=fill_value, base=0,
                                   pattern=[[-sign, P]], channel_multiplier=sign).then_inc(fills, 1)

            for tile, value in ((ident, 1.0), (ident_h, 1.0), (neg_m, 0.0), (neg_s, 0.0), (before, 1.0),
                                (neg_tri, -1.0), (ones, 1.0), (tri, 1.0), (valid, 1.0),
                                (invalid, 0.0), (eps, EPS), (one, 1.0)):
                pool.memset(tile[:, :], value)
            pool.memset(neg_blk[:, :, :], -1.0)
            pool.iota(iota_i[:, :], [[1, TOPK]], base=0, channel_multiplier=0)
            pool.memset(state[:, :, :], 0.0).then_inc(fill, 1)
            pool.wait_ge(fill, 1)
            select(ident, 1, ALU.is_equal, 0.0)
            select(ident_h, 1, ALU.is_equal, 0.0)
            select(neg_m, -1, ALU.is_ge, NEG)
            select(neg_s, -1, ALU.is_gt, NEG)
            select(before, -1, ALU.is_gt, 0.0)
            select(neg_tri, 1, ALU.is_ge, 0.0)
            select(tri, -1, ALU.is_ge, 0.0)
            pool.affine_select(out=valid[:, :], in_=valid[:, :], compare_op=ALU.is_ge, fill=0.0,
                               base=-(P - N_META), pattern=[[0, 1]], channel_multiplier=1).then_inc(fills, 1)
            pool.affine_select(out=invalid[:, :], in_=invalid[:, :], compare_op=ALU.is_ge, fill=NEG,
                               base=-(P - N_META), pattern=[[0, 1]], channel_multiplier=1).then_inc(fills, 1)
            pool.affine_select(out=neg_blk[:, :, :], in_=neg_blk[:, :, :], compare_op=ALU.is_equal, fill=0.0,
                               base=0, pattern=[[-1, MH], [0, P]], channel_multiplier=1).then_inc(fills, 1)
            pool.tensor_copy(iota16[:, :], iota_i[:, :]).then_inc(fills, 1)

            def gather(ring, s, landed, free, table, idx, jj, n):
                pool.wait_ge(free, n + 1)
                pool.sem_inc(pool_turn, 1)
                pool.indirect_dma_start(out=ring[:, s, :], out_offset=None, in_=table,
                                        in_offset=bass.IndirectOffsetOnAxis(ap=idx[:, jj:jj + 1], axis=0)
                                        ).then_inc(landed[s], 16)

            def picks(T, g, q, dot, sums):
                a, b = (T - 1) * GROUPS + g, (T - 2) * GROUPS + g
                if dot:
                    pool.tensor_copy(idx_u[q][:, :], chosen_u[:, bass.ds(g * GROUP, GROUP)]).then_inc(
                        idx_u_copied, 1)
                if sums:
                    pool.tensor_copy(idx_v[q][:, :], chosen_v[:, bass.ds(g * GROUP, GROUP)]).then_inc(
                        idx_v_copied, 1)
                if dot:
                    pool.wait_ge(idx_u_copied, a + 1)
                if sums:
                    pool.wait_ge(idx_v_copied, b + 1)
                pool.sem_inc(pool_turn, 1)
                for jj in range(GROUP):
                    if dot:
                        gather(ring_u, jj % RING_U, u_landed, u_free, expert_u, idx_u[q], jj, a * GROUP + jj)
                    if sums:
                        gather(ring_v, jj % RING_V, v_landed, v_free, expert_v, idx_v[q], jj, b * GROUP + jj)

            def step(T, dot=True, sums=True):
                if sums:
                    pool.tensor_copy(chosen_v[:, :], chosen_u[:, :]).then_inc(chosen_moved, 1)
                    pool.wait_ge(chosen_moved, 2 * T - 2)
                if dot:
                    pool.wait_ge(idx_ready, PH * T)
                    pool.sem_inc(pool_turn, 1)
                    pool.tensor_copy(chosen_u[:, :], chosen[:, :]).then_inc(chosen_moved, 1)
                    pool.wait_ge(chosen_moved, 2 * T - 1)
                    pool.sem_inc(pool_turn, 1)
                with pool.Fori(0, PH) as h:
                    for q in range(2):
                        picks(T, 2 * h + q, q, dot, sums)

            step(1, sums=False)
            with pool.Fori(2, LAST + 1) as T:
                step(T)
            step(LAST + 1, dot=False)

        def expert_step(eng, T, group, work, mix, route):
            M, R = T + 2, T + 1

            def at_picks(g):
                found = {}
                for key, f in work["route"].items():
                    if route and key[0] == g:
                        found.setdefault(key[1], []).append(lambda f=f: f(R))
                for key, f in work["mix"].items():
                    if mix and key[0] == g:
                        found.setdefault(key[1], []).append(lambda f=f: f(M))
                return found

            def in_middle(i, h):
                found = {}
                for jj, f in work["blocks"].items():
                    if i is not None:
                        found.setdefault(jj, []).append(lambda f=f: f(M, i))
                for jj, f in work["heads"].items():
                    if h is not None:
                        found.setdefault(jj, []).append(lambda f=f: f(R, h, mix))
                return found

            for g in range(PRE):
                group(T, g, at_picks(g))
            if isinstance(T, int) and T == 0:
                first_step(eng, M, group, work, in_middle)
                return
            if mix:
                with eng.Fori(1, M + 1) as i:
                    group(T, i + (PRE - 1), in_middle(i, i - 1))
                if not (isinstance(M, int) and M == LAST):
                    with eng.Fori(0, PH - M) as n:
                        h = n + M
                        if not isinstance(h, int):
                            h = nc.s_assert_within(h, 0, PH - 1, skip_runtime_bounds_check_because="n + M < PH")
                        group(T, h + PRE, in_middle(None, h))
            else:
                with eng.Fori(0, PH) as h:
                    group(T, h + PRE, in_middle(None, h if route else None))
            for g in range(PRE + MIDDLE, GROUPS):
                group(T, g, at_picks(g))

        def first_step(eng, M, group, work, in_middle):
            with eng.Fori(1, M + 1) as i:
                group(0, i + (PRE - 1), in_middle(i, i - 1))
            for n, h in enumerate(range(M, PH)):
                found = {}
                for (g, jj), f in work["mix"].items():
                    if g == PRE + MIDDLE + n and (g, jj) < N2_MOVES:
                        found[jj] = [lambda f=f: f(M)]
                for jj, fs in in_middle(None, h).items():
                    found.setdefault(jj, []).extend(fs)
                group(0, h + PRE, found)
            for key in sorted(work["route"]):
                work["route"][key](1)
            for key in sorted(work["mix"]):
                if key >= N2_MOVES:
                    work["mix"][key](M)

        def expert_steps(eng, group, end, begin, work):
            def one(T, mix, route, dot, sums):
                begin(T, route, dot, sums)
                expert_step(eng, T, lambda *a: group(*a, dot=dot, sums=sums), work, mix, route)
                end(T, dot, sums)

            one(0, True, True, False, False)
            one(1, True, True, True, False)
            one(2, True, True, True, True)
            with eng.Fori(3, LAST - 2) as T:
                one(T, True, True, True, True)
            one(LAST - 2, True, True, True, True)
            one(LAST - 1, False, True, True, True)
            one(LAST, False, False, True, True)
            one(LAST + 1, False, False, False, True)

        def mix_first(work, fill_in=None):
            fill_in = fill_in or {}
            steps = [(key, work["mix"][key]) for key in sorted(work["mix"]) if key[0] < PRE]
            steps += [(jj, lambda T, f=work["blocks"][jj]: f(T, 1)) for jj in sorted(work["blocks"])]
            steps += [(key, work["mix"][key]) for key in sorted(work["mix"]) if key[0] >= PRE]
            for key, step in steps:
                step(1)
                if key in fill_in:
                    work["fold"](*fill_in[key])

        FOLDS = [(0, 10), (10, 18), (18, 22), (22, 26), (26, 4 * PH)]

        @block.scalar
        def _(act):
            def copy(out_, in_, scale=1.0):
                return nc.scalar.activation(out_, in_, ACT.Copy, scale=scale)

            act.wait_ge(fills, FILLS)
            act.wait_ge(consts_in, 16 * N_CONSTS)
            Lp = Links(act, act_p, 1)

            def norms(T, p, k):
                act.wait_ge(x_landed[p], 16 * (k + 1))
                wait(act, summed, T)
                nc.scalar.activation(sqT, xT_sb[p], ACT.Square).then_inc(squared, 1)
                act.wait_ge(summed, T + 1)
                wait(act, n_ready, T - 1)
                Lp.at(T)
                Lp(nc.scalar.activation(rsT[p], sum_psum, ACT.Ln, scale=1.0 / D, bias=eps[:, :]))
                nc.scalar.activation(rsT[p], rsT[p], ACT.Exp, scale=-0.5).then_inc(rs_ready, 1)

            def tile_step(T, p, k):
                lead = isinstance(T, int) and T == 0
                wait(act, stored[p], 32 * k)
                act.wait_ge(unit_done["u"], T + 1)
                wait(act, hist_moved, T + 1)
                copy(ucat[:, :, 3:], b4(2)).then_inc(unit_taken["u"], 1)
                if not (isinstance(T, int) and T == LAST):
                    norms(T + 1, 1 - p, k + p)
                if not lead:
                    act.wait_ge(unit_done["qs"], T)
                    copy(slot(p, "qs"), bank[4][:, :], SD ** -0.5).then_inc(unit_taken["qs"], 1)
                    act.wait_ge(unit_done["so"], T)
                    nc.scalar.activation(slot(p, "so"), bank[6][:, :], ACT.Exp, scale=-1.0).then_inc(
                        unit_taken["so"], 1)
                act.wait_ge(conv_ready, T + 1)
                nc.scalar.activation(sig, conv, ACT.Exp, scale=-1.0).then_inc(conv_exp, 1)
                act.wait_ge(unit_done["vs"], T + 1)
                copy(slot(p, "vs"), bank[7][:, :]).then_inc(unit_taken["vs"], 1)
                act.sem_inc(act_turn, 1)
                act.wait_ge(unit_taken["vs"], T + 1)
                act.sem_inc(staged_act, 1)

            norms(0, 0, 0)
            project(act, tile_step)

            act.wait_ge(unit_taken["gates"], TILES)
            act.wait_ge(stored[0], 32 * 5)
            act.wait_ge(stored[1], 32 * 4)
            nc.scalar.activation(tmp36.rearrange("p (t h) -> p t h", t=TILES), graw[:, :, MH:2 * MH],
                                 ACT.Abs).then_inc(gate_act, 1)
            act.wait_ge(gate_act, 1)
            nc.scalar.activation(tmp36, tmp36, ACT.Exp, scale=-1.0).then_inc(gate_act, 1)
            act.wait_ge(gate_act, 2)
            nc.scalar.activation(tmp36, tmp36, ACT.Ln, bias=one[:, :]).then_inc(gate_act, 1)
            def fold(a, b):
                for u in range(a, b):
                    act.wait_ge(fold_done, u + 1)
                    copy(w_qT[:, u // 2, u % 2 * 512:u % 2 * 512 + 512], acc[:, u % 2, :]).then_inc(fold_copied, 1)

            fold(*FOLDS[0])
            act.wait_ge(rows_ready, 1)
            nc.scalar.activation(rows_wi, rows_wi, ACT.Exp)
            nc.scalar.activation(rows_em, rows_em, ACT.Exp, scale=-1.0)
            nc.scalar.activation(rows_ws, rows_ws, ACT.Exp)
            nc.scalar.activation(dec_row, dec_row, ACT.Exp).then_inc(gate_act, 1)

            def copy_qk(T):
                act.wait_ge(qk_done, T + 1)
                wait(act, y_ready, T - 4)
                copy(q_m, b4(2))
                copy(k_m, b4(3), MD ** -0.5).then_inc(qk_copied, 1)

            def exp_w(T):
                act.wait_ge(se_done, T)
                act.wait_ge(now_ready, T + 1)
                wait(act, out_stored, 16 * (T - 4))
                for h in range(MH):
                    last = nc.scalar.activation(wexp[:, h, :], b4(3)[:, h, :], ACT.Exp, bias=now[:, 0, h:h + 1])
                last.then_inc(wexp_ready, 1)

            def scale_inter(T):
                act.wait_ge(hh_done, T)
                wait(act, n2T_done, T - 1)
                for h in range(MH):
                    last = copy(inter[:, h, :], b2(6 + h // 2)[:, h % 2, :], now[:, 1, h:h + 1])
                last.then_inc(inter_ready, 1)

            Lf = Links(act, act_f, 1)

            def rsqrt(out_, in_, n):
                Lf(nc.scalar.activation(out_, in_, ACT.Ln, scale=1.0 / n, bias=eps[:, :]))
                return nc.scalar.activation(out_, out_, ACT.Exp, scale=-0.5)

            def rstd_m(T):
                Lf.at(T - 1)
                act.wait_ge(var_ready, T)
                rsqrt(rstd, var, MD).then_inc(rstd_ready, 1)

            def skip_m(T):
                act.wait_ge(dstate_done, T + 1)
                for h in range(MH):
                    last = copy(skip_c[:, h, :], cT[:, h, :], skip_g[:, h:h + 1])
                last.then_inc(skip_ready, 1)

            Ls = Links(act, act_s, 2)

            def ln_z(T, i):
                c = units_before(T) + i
                Ls.at(c)
                if diagonal(i):
                    act.wait_ge(ym_ready, T)
                wait(act, av_done, c)
                for hg in range(2):
                    act.wait_ge(z_done, 2 * c + hg + 1)
                    last = nc.scalar.activation(zl[hg], bank[2 + hg][:, :], ACT.Abs)
                Ls(last)
                for hg in range(2):
                    last = nc.scalar.activation(zl[hg], zl[hg], ACT.Exp, scale=-1.0)
                Ls(last)
                for hg in range(2):
                    nc.scalar.activation(zl[hg], zl[hg], ACT.Ln, bias=one[:, :]).then_inc(ln_ready, 1)

            def exp_a(T, i):
                c = units_before(T) + i
                for hg in range(2):
                    act.wait_ge(s_done, 2 * c + hg + 1)
                    act.wait_ge(sp_ready, 2 * c + hg + 1)
                    nc.scalar.activation(zl[hg], bank[2 + hg][:, :], ACT.Exp).then_inc(a_ready, 1)

            def square_o(T):
                act.wait_ge(av_done, units_before(T + 1))
                nc.scalar.activation(osq, bank[5][:, :], ACT.Square).then_inc(osq_ready, 1)

            Lo = Links(act, act_o, 1)

            def rs_o(T):
                act.wait_ge(oss_ready, T)
                Lo.at(T - 1)
                Lo(nc.scalar.activation(ors, oss, ACT.Ln, scale=1.0 / SD, bias=eps[:, :]))
                nc.scalar.activation(ors, ors, ACT.Exp, scale=-0.5).then_inc(ors_ready, 1)

            def copy_ys(T):
                act.wait_ge(onT_done, T)
                for h in range(4):
                    last = copy(yT[:, 4 + h, :], b4(2)[:, h, :], sb_g[:, h:h + 1])
                last.then_inc(ys_ready, 1)

            Lh = Links(act, act_h, 2)

            def rs_h(T):
                act.wait_ge(h_ready, T)
                Lh.at(T - 1)
                Lh(nc.scalar.activation(square_out, hx, ACT.Square, accum_out=hss))
                Lh(nc.scalar.activation(hrs, hss, ACT.Ln, scale=1.0 / D, bias=eps[:, :]))
                nc.scalar.activation(hrs, hrs, ACT.Exp, scale=-0.5).then_inc(hrs_ready, 1)

            def copy_n2T(T):
                act.wait_ge(n2T_done, T)
                wait(act, scores_done, PH * (T - 1))
                for k in range(KC):
                    last = copy(n2T[:, k, :], b4(2 + k // 4)[:, k % 4, :], g_ffn[:, k:k + 1])
                last.then_inc(n2T_copied, 1)

            def exp_soft(T):
                act.wait_ge(soft_in, T)
                nc.scalar.activation(gate_next[:, :, :], gate_next[:, :, :], ACT.Exp).then_inc(soft_exp, 1)

            work = {
                "mix": {(0, 2): copy_qk, (0, 5): exp_w, (1, 1): scale_inter, (1, 4): rstd_m, (1, 6): skip_m,
                        (2, 1): lambda T: ln_z(T, 0), (2, 5): lambda T: exp_a(T, 0), (11, 0): square_o,
                        (11, 2): rs_o, (11, 5): copy_ys, (12, 7): rs_h, (13, 7): copy_n2T},
                "route": {(11, 1): exp_soft},
                "blocks": {1: ln_z, 5: exp_a},
                "heads": {},
                "fold": fold,
            }
            mix_first(work, {(1, 1): FOLDS[1], (2, 1): FOLDS[2], 1: FOLDS[3], (12, 7): FOLDS[4]})

            def begin(T, route, dot, sums):
                if route:
                    wait(act, xs_ready, 2 * T)
                    act.wait_ge(n2_back, T + 1)
                    copy(n2_next[:, 0:512], bank[2][:, :])
                    copy(n2_next[:, 512:1024], bank[3][:, :]).then_inc(n2_moved, 1)
                if sums:
                    act.wait_ge(wgt_ready, T - 1)

            def group(T, g, at_pick, dot, sums):
                n = ((T - 2) * GROUPS + g) * GROUP
                fixed = isinstance(g, int)
                if sums and not fixed:
                    act.wait_ge(diag_ready, n)
                    act.sem_inc(act_turn, 1)
                    copy(wgt8[:, :], wgt[:, bass.ds(g * GROUP, GROUP)]).then_inc(wgt_moved, 1)
                    act.wait_ge(wgt_moved, (T - 2) * MIDDLE + g - (PRE - 1))
                for jj in range(GROUP):
                    if sums:
                        act.wait_ge(v_free, n + jj + 1 + RING_V - 4)
                        col = wgt[:, g * GROUP + jj:g * GROUP + jj + 1] if fixed else wgt8[:, jj:jj + 1]
                        copy(diag[:, jj % 4, :], ident[:, :], col).then_inc(diag_ready, 1)
                    for f in at_pick.get(jj, ()):
                        f()

            Ly = Links(act, act_y, 2)

            def end(T, dot, sums):
                if dot:
                    act.wait_ge(u_free, RING_U + T * NJ)
                    act.wait_ge(dots_moved, T * MIDDLE)
                    nc.scalar.activation(dots[:, :], dots[:, :], ACT.Gelu).then_inc(gelu_ready, 1)
                if sums:
                    act.wait_ge(acc_read, T - 1)
                    Ly.at(T - 2)
                    Ly(nc.scalar.activation(diag[:, :, :].bitcast(BF16)[:, :, 0:P * 2].rearrange("p a b -> p (a b)"),
                                            y_res, ACT.Square, accum_out=yss))
                    Ly(nc.scalar.activation(yrs, yss, ACT.Ln, scale=1.0 / D, bias=eps[:, :]))
                    nc.scalar.activation(yrs, yrs, ACT.Exp, scale=-0.5).then_inc(yrs_ready, 1)

            expert_steps(act, group, end, begin, work)

        @block.vector
        def _(dve):
            def TT(out_, a, b, op):
                return nc.vector.tensor_tensor(out_, a, b, op)

            def TS(out_, a, s1, op0, s2=None, op1=None):
                if op1 is None:
                    return nc.vector.tensor_scalar(out_, a, s1, None, op0)
                return nc.vector.tensor_scalar(out_, a, s1, s2, op0, op1)

            def STT(out_, a, s, b, op0, op1):
                return nc.vector.scalar_tensor_tensor(out=out_, in0=a, scalar=s, in1=b, op0=op0, op1=op1)

            nc.vector.memset(ucat[:, :, 0:3], 0.0).then_inc(hist_moved, 1)
            dve.wait_ge(fills, FILLS)
            dve.wait_ge(consts_in, 16 * N_CONSTS)

            def normalise(T, p):
                dve.wait_ge(rs_ready, T + 1)
                wait(dve, unit_done["gates"], T - 1)
                for k in range(KC):
                    last = STT(nT[p][:, k, :], xT_sb[p][:, k, :], g_mix[:, k:k + 1], rsT[p], ALU.mult, ALU.mult)
                last.then_inc(n_ready, 1)

            Lp = Links(dve, dve_p, CONV + 5)

            def tile_step(T, p, k):
                lead = isinstance(T, int) and T == 0
                if not (isinstance(T, int) and T == LAST):
                    normalise(T + 1, 1 - p)
                Lp.at(T)
                dve.wait_ge(unit_taken["u"], T + 1)
                for w in range(CONV):
                    for h in range(MH):
                        c, tap = conv[:, h, :], conv_w[:, h * CONV + w:h * CONV + w + 1]
                        if w == 0:
                            last = TS(c, ucat[:, h, 0:P], tap, ALU.mult, conv_b[:, h:h + 1], ALU.add)
                        else:
                            last = STT(c, ucat[:, h, w:w + P], tap, c, ALU.mult, ALU.add)
                    if w == CONV - 1:
                        last.then_inc(conv_ready, 1)
                        dve.wait_ge(conv_ready, T + 1)
                        dve.sem_inc(dve_p, 1)
                        Lp.k += 1
                    else:
                        Lp(last)
                nc.vector.tensor_copy(ucat[:, :, 0:3], ucat[:, :, P:P + 3]).then_inc(hist_moved, 1)
                wait(dve, stored[p], 32 * k)
                dve.wait_ge(unit_done["ks"], T + 1)
                nc.vector.tensor_copy(slot(p, "ks"), bank[3][:, :]).then_inc(unit_taken["ks"], 1)
                dve.wait_ge(unit_done["v"], T + 1)
                nc.vector.tensor_copy(slot(p, "v"), bank[5][:, :]).then_inc(unit_taken["v"], 1)
                dve.wait_ge(conv_exp, T + 1)
                Lp(TS(sig, sig, 1.0, ALU.add))
                Lp(nc.vector.reciprocal(sig, sig))
                Lp(TT(slot4(p, "c"), conv, sig, ALU.mult))
                if lead:
                    dve.sem_inc(dve_p, 2)
                    Lp.k += 2
                else:
                    dve.wait_ge(unit_taken["so"], T)
                    Lp(TS(slot(p, "so"), slot(p, "so"), 1.0, ALU.add))
                    Lp(nc.vector.reciprocal(slot(p, "so"), slot(p, "so")))
                dve.wait_ge(unit_done["gates"], T + 1)
                TT(graw[:, bass.ds(T, 1), :].rearrange("p a b -> p (a b)"), gate_psum, gbias[:, :],
                   ALU.add).then_inc(unit_taken["gates"], 1)
                dve.wait_ge(unit_taken["gates"], T + 1)
                dve.sem_inc(staged_dve, 1)

            normalise(0, 0)
            project(dve, tile_step)

            dve.wait_ge(stored[0], 32 * 5)
            dve.wait_ge(stored[1], 32 * 4)
            n_link = [0]

            def L(ins):
                n_link[0] += 1
                ins.then_inc(gate_dve, 1)
                dve.wait_ge(gate_dve, n_link[0])

            g9 = graw[:, :, :]

            def v9(ap):
                return ap.rearrange("p (t h) -> p t h", t=TILES)

            L(nc.vector.tensor_copy(v9(li), g9[:, :, 0:MH]))
            L(TS(li[:, 0:MH], li[:, 0:MH], valid[:, :], ALU.mult, invalid[:, :], ALU.add))
            dve.wait_ge(gate_act, 3)
            L(STT(v9(lf), g9[:, :, MH:2 * MH], 0.0, v9(tmp36), ALU.min, ALU.subtract))
            TS(lf[:, 0:MH], lf[:, 0:MH], valid[:, :], ALU.mult).then_inc(gate_in, 1)
            dve.wait_ge(gate_pe, 1)
            L(TT(cols[:, 0, :], li, bank[2][:, 0:W36], ALU.subtract))
            L(nc.vector.tensor_copy(tmp36, bank[2][:, 0:W36]))
            dve.sem_inc(gate_in, 1)
            dve.wait_ge(gate_pe, 2)
            for i in range(3):
                a, b = 512 * i, min(512 * (i + 1), TILES * P)
                L(nc.vector.tensor_copy(rows_a[:, a:b], bank[3 + i][0:MH, 0:b - a]))
            for i in range(3):
                a, b = 512 * i, min(512 * (i + 1), TILES * P)
                L(nc.vector.tensor_copy(rows_b[:, a:b], bank[(6, 7, 2)[i]][0:MH, 0:b - a]))
            L(nc.vector.memset(m_row[:, 0:1], 0.0))
            for T in range(TILES):
                r = rows_a[:, T * P:(T + 1) * P]
                L(nc.vector.tensor_tensor_scan(rows_M[:, T * P:(T + 1) * P], r, r, m_row[:, T:T + 1],
                                               ALU.max, ALU.max))
                e = (T + 1) * P
                L(TT(m_row[:, T + 1:T + 2], rows_b[:, e - 1:e], rows_M[:, e - 1:e], ALU.add))
            dve.sem_inc(top_ready, 1)

            def r3(ap):
                return ap.rearrange("p (t s) -> p t s", t=TILES)

            def spread(ap):
                return wide(ap, [MH, TILES, P])

            M_end = r3(rows_M)[:, :, P - 1]
            TT(r3(rows_wi), spread(m_row[:, 0:TILES]), r3(rows_M), ALU.subtract)
            TT(rows_em, rows_b, rows_M, ALU.add)
            TT(r3(rows_ws), r3(rows_a), spread(M_end), ALU.subtract)
            L(TT(dec_row, m_row[:, 0:TILES], M_end, ALU.subtract))
            dve.sem_inc(rows_ready, 1)
            dve.wait_ge(gate_act, 4)
            L(STT(dec_blk.rearrange("p (t h) -> p t h", t=TILES), wide(dec_row, [MH, TILES, MH]), -1.0,
                  neg_blk[:, :, 0].unsqueeze(1).broadcast_to([MH, TILES, MH]), ALU.mult, ALU.mult))
            dve.sem_inc(gate_in, 1)
            dve.wait_ge(gate_pe, 3)
            L(nc.vector.tensor_copy(cols[:, 1:4, :], bank[3][:, 0:3 * W36].rearrange("p (a b) -> p a b", a=3)))
            L(nc.vector.tensor_copy(cols[:, 4, :], bank[4][:, 0:W36]))
            L(nc.vector.memset(vx[:, :, MD:MD + 1], 1.0))
            dve.sem_inc(gates_ready, 1)

            Lm = Links(dve, dve_m, 9)

            def set_now(T):
                lead = isinstance(T, int) and T == 0
                wait(dve, state_ready, T)
                dve.sem_inc(dve_turn, 1)
                nc.vector.tensor_copy(now[:, :, :], cols[:, :, bass.ds(T * MH, MH)]).then_inc(now_ready, 1)
                dve.wait_ge(now_ready, T + 1)
                dve.wait_ge(mix_in, 32 + 64 * T)
                if not lead:
                    wait(dve, n2T_done, T - 1)
                    TT(m_blk, m_top[:, :].unsqueeze(1).broadcast_to([MH, MH, P]), neg_blk[:, :, :],
                       ALU.mult).then_inc(m_blk_ready, 1)

            def make_kw(T):
                dve.wait_ge(qk_done, T + 1)
                wait(dve, out_stored, 16 * (T - 4))
                for h in range(MH):
                    last = TS(kw[:, h, :], b4(4)[:, h, :], MD ** -0.5, ALU.mult, now[:, 3, h:h + 1], ALU.mult)
                last.then_inc(kw_ready, 1)

            def make_p(T):
                dve.wait_ge(wexp_ready, T)
                TT(wexp, b4(2), wexp, ALU.mult).then_inc(p_ready, 1)

            def update_state(T):
                dve.wait_ge(dstate_done, T + 1)
                for h in range(MH):
                    last = STT(state[:, h, :], state[:, h, :], now[:, 4, h:h + 1], b2(2 + h // 2)[:, h % 2, :],
                               ALU.mult, ALU.add)
                last.then_inc(state_ready, 1)

            def make_h(T):
                Lm.at(T - 1)
                dve.wait_ge(inter_ready, T)
                for i in range(2):
                    last = TT(nd[:, 2 * i:2 * i + 2, :], inter[:, 2 * i:2 * i + 2, :], b2(4 + i), ALU.add)
                Lm(last)
                update_state(T)
                Lm(STT(den, nd[:, :, MD], -1.0, nd[:, :, MD], ALU.mult, ALU.max))
                Lm(TT(den, den, now[:, 2, :], ALU.max))
                Lm(nc.vector.reciprocal(den, den))
                for h in range(MH):
                    last = STT(hb[:, h, :], nd[:, h, 0:MD], den[:, h:h + 1], so[:, h, :], ALU.mult, ALU.mult)
                Lm(last)
                Lm(nc.vector.tensor_reduce(mean, hb, AX_X, ALU.add))
                Lm(TS(mean, mean, -1.0 / MD, ALU.mult))
                Lm(TT(hb, hb, wide(mean, [P, MH, MD]), ALU.add))
                Lm(TT(hsq, hb, hb, ALU.mult))
                nc.vector.tensor_reduce(var, hsq, AX_X, ALU.add).then_inc(var_ready, 1)

            def make_hn(T):
                dve.wait_ge(rstd_ready, T)
                TT(hb, hb, wide(rstd, [P, MH, MD]), ALU.mult).then_inc(hn_ready, 1)

            def make_ym(T):
                dve.wait_ge(hnT_done, T)
                dve.wait_ge(skip_ready, T)
                for h in range(MH):
                    last = STT(yT[:, h, :], b4(4)[:, h, :], gn_g[:, h:h + 1], skip_c[:, h, :], ALU.mult, ALU.add)
                last.then_inc(ym_ready, 1)

            Lz = Links(dve, dve_s, 1)

            def make_sp(T, i):
                c = units_before(T) + i
                Lz.at(c)
                for hg in range(2):
                    dve.wait_ge(ln_ready, 2 * c + hg + 1)
                    last = STT(sp_[hg], bank[2 + hg][:, :], 0.0, zl[hg], ALU.max, ALU.add)
                    if not diagonal(i):
                        last.then_inc(sp_ready, 1)
                if not diagonal(i):
                    dve.sem_inc(dve_s, 1)
                    Lz.k += 1
                    return
                Lz(last)
                for hg in range(2):
                    v = sp_[hg].rearrange("p (c t) -> p c t", c=SHP)
                    TT(v, v, before[:, :].unsqueeze(1).broadcast_to([P, SHP, P]), ALU.mult).then_inc(sp_ready, 1)

            def add_later(T, i):
                c = units_before(T) + i
                dve.wait_ge(s_done, 2 * c + 2)
                dve.wait_ge(sp_ready, 2 * c + 2)
                for hg in range(2):
                    if diagonal(i):
                        last = TS(later[hg], sp_[hg], -1.0, ALU.mult)
                    else:
                        last = TT(later[hg], later[hg], sp_[hg], ALU.subtract)
                last.then_inc(later_ready, 1)
                dve.wait_ge(later_ready, c + 1)

            def sum_o(T):
                dve.wait_ge(osq_ready, T)
                nc.vector.tensor_reduce(oss, osq.rearrange("p (h d) -> p h d", h=SH), AX_X, ALU.add).then_inc(
                    oss_ready, 1)

            def make_on(T):
                dve.wait_ge(ors_ready, T)
                TT(on.rearrange("p (h d) -> p h d", h=SH), bank[5][:, :].rearrange("p (h d) -> p h d", h=SH),
                   wide(ors, [P, SH, SD]), ALU.mult).then_inc(on_ready, 1)

            def make_h2(T):
                dve.wait_ge(mixed, T)
                dve.wait_ge(x_in, 16 * T)
                for i in range(2):
                    last = TT(hx[:, 512 * i:512 * i + 512], hx[:, 512 * i:512 * i + 512], bank[(4, 7)[i]][:, :],
                              ALU.add)
                last.then_inc(h_ready, 1)

            def make_n2(T):
                dve.wait_ge(hrs_ready, T)
                dve.wait_ge(h_stored, 16 * T)
                TS(hx, hx, hrs, ALU.mult).then_inc(n2_ready, 1)

            Lt = Links(dve, dve_t, 9)

            def LT(ins):
                Lt(ins)
                dve.sem_inc(dve_turn, 1)

            def top16(lists):
                for values, _, src, _ in lists:
                    last = nc.vector.max(values[:, 0:8], src)
                LT(last)
                for values, indices, src, spare in lists:
                    nc.vector.max_index(indices[:, 0:8], values[:, 0:8], src)
                    last = nc.vector.match_replace(spare, values[:, 0:8], src, LOWEST)
                LT(last)
                for values, _, _, spare in lists:
                    last = nc.vector.max(values[:, 8:16], spare)
                LT(last)
                for values, indices, _, spare in lists:
                    last = nc.vector.max_index(indices[:, 8:16], values[:, 8:16], spare)
                LT(last)

            def halves(T, h, mix):
                turn = (T - 1) * PH + h
                Lt.at(turn)
                dve.wait_ge(scores_done, turn + 1)
                dve.sem_inc(dve_turn, 1)
                top16([(srt[:, p, :], sri[:, p, :], bank[6][:, p * NKEY:(p + 1) * NKEY],
                        rest[:, p * NKEY:(p + 1) * NKEY]) for p in range(2)])
                dve.sem_inc(scores_free, 1)

            def pair_sums(T, h, mix):
                LT(TT(cand[:, :, :], wide(srt[:, 0, :], [P, TOPK, TOPK]),
                      srt[:, 1, :].unsqueeze(1).broadcast_to([P, TOPK, TOPK]), ALU.add))
                top16([(best_h[:, :], pos[:, :], cand[:, :, :].rearrange("p a b -> p (a b)"), rest[:, :])])

            def choose(T, h, mix):
                E = 4 * ((T - 1) * PH + h)
                nc.vector.tensor_copy(best[:, :, :].rearrange("p a b -> p (a b)")[:, bass.ds(h * TOPK, TOPK)],
                                      best_h[:, :])
                TS(half[:, 0, :], pos[:, :], 4, ALU.logical_shift_right)
                TS(half[:, 1, :], pos[:, :], 15, ALU.bitwise_and).then_inc(dve_e, 1)
                dve.wait_ge(dve_e, E + 1)
                r2 = [rest[:, :].rearrange("p (k i) -> p k i", k=TOPK), cand[:, :, :]]
                for q in range(2):
                    last = TT(r2[q], wide(half[:, q, :], [P, TOPK, TOPK]),
                              iota16[:, :].unsqueeze(1).broadcast_to([P, TOPK, TOPK]), ALU.is_equal)
                last.then_inc(dve_e, 1)
                dve.wait_ge(dve_e, E + 2)
                for q in range(2):
                    last = TT(r2[q], r2[q], sri[:, q, :].unsqueeze(1).broadcast_to([P, TOPK, TOPK]), ALU.mult)
                last.then_inc(dve_e, 1)
                dve.wait_ge(dve_e, E + 3)
                for q in range(2):
                    last = nc.vector.tensor_reduce(sel[:, q, :], r2[q], AX_X, ALU.add)
                last.then_inc(dve_e, 1)
                dve.wait_ge(dve_e, E + 4)
                dve.sem_inc(dve_turn, 1)
                if not isinstance(T, int) or T > 1:
                    dve.wait_ge(chosen_moved, 2 * T - 3)
                    dve.sem_inc(dve_turn, 1)
                STT(chosen[:, bass.ds(h * TOPK, TOPK)], sel[:, 0, :], float(NKEY), sel[:, 1, :],
                    ALU.mult, ALU.add).then_inc(idx_ready, 1)

            def soften(T):
                dve.wait_ge(idx_ready, PH * T)
                dve.sem_inc(dve_turn, 1)
                TT(gate_next[:, :, :], best[:, :, :], best[:, :, 0:1].broadcast_to([P, PH, TOPK]),
                   ALU.subtract).then_inc(soft_in, 1)

            Lg = Links(dve, dve_g, 3)

            def divide(T):
                dve.wait_ge(soft_exp, T)
                Lg.at(T - 1)
                Lg(nc.vector.tensor_reduce(gsum[:, 0, :], gate_next[:, :, :], AX_X, ALU.add))
                Lg(nc.vector.reciprocal(gsum[:, 1, :], gsum[:, 0, :]))
                Lg(TT(gate_next[:, :, :], gate_next[:, :, :], wide(gsum[:, 1, :], [P, PH, TOPK]), ALU.mult))

            work = {
                "mix": {(0, 0): set_now, (0, 3): make_kw, (0, 6): make_p, (1, 2): make_h, (1, 5): make_hn,
                        (1, 7): make_ym, (2, 2): lambda T: make_sp(T, 0), (2, 5): lambda T: add_later(T, 0),
                        (11, 1): sum_o, (11, 3): make_on, (12, 5): make_h2, (13, 3): make_n2},
                "route": {(11, 0): soften, (11, 5): divide},
                "blocks": {2: make_sp, 5: add_later},
                "heads": {3: halves, 6: pair_sums, 7: choose},
            }

            dve.sem_inc(scores_free, 1)
            set_now(0)
            make_kw(0)
            update_state(0)
            mix_first(work)

            def begin(T, route, dot, sums):
                if dot:
                    wait(dve, u_free, RING_U + (T - 1) * NJ)
                    dve.wait_ge(n2_moved, T)
                    dve.sem_inc(dve_turn, 1)
                    nc.vector.tensor_copy(xs[:, :], n2_next[:, :]).then_inc(xs_ready, 1)
                    nc.vector.tensor_copy(gate_now[:, :], gate_next[:, :, :].rearrange("p a b -> p (a b)")).then_inc(
                        xs_ready, 1)
                    dve.wait_ge(xs_ready, 2 * T)

            def group(T, g, at_pick, dot, sums):
                a = (T - 1) * GROUPS + g
                fixed = isinstance(g, int)
                for jj in range(GROUP):
                    if dot:
                        dve.wait_ge(u_landed[jj % RING_U], ((T - 1) * GROUPS + g) * (16 * GROUP // RING_U)
                                    + 16 * (jj // RING_U + 1))
                        s = ring_u[:, jj % RING_U, :]
                        col = dots[:, g * GROUP + jj:g * GROUP + jj + 1] if fixed else dots8[:, jj:jj + 1]
                        nc.vector.tensor_tensor_reduce(s, s, xs[:, :], 1.0, 0.0, ALU.mult, ALU.add,
                                                       col).then_inc(u_free, 1)
                    for f in at_pick.get(jj, ()):
                        f()
                if dot and not fixed:
                    dve.wait_ge(u_free, RING_U + (a + 1) * GROUP)
                    dve.sem_inc(dve_turn, 1)
                    nc.vector.tensor_copy(dots[:, bass.ds(g * GROUP, GROUP)], dots8[:, :]).then_inc(dots_moved, 1)
                    dve.wait_ge(dots_moved, (T - 1) * MIDDLE + g - (PRE - 1))

            def end(T, dot, sums):
                if dot:
                    dve.wait_ge(gelu_ready, T)
                    TT(wgt[:, :], dots[:, :], gate_now[:, :], ALU.mult).then_inc(wgt_ready, 1)
                    dve.wait_ge(wgt_ready, T)
                if sums:
                    dve.wait_ge(v_free, RING_V + (T - 1) * NJ)
                    dve.wait_ge(res_in, 16 * (T - 1))
                    TT(y_res, acc[:, :, :].rearrange("p a b -> p (a b)"), y_res, ALU.add).then_inc(
                        acc_read, 1)
                    dve.wait_ge(yrs_ready, T - 1)
                    dve.wait_ge(acc_read, T - 1)
                    dve.wait_ge(g_fin_in, 16 * (T - 1) if not isinstance(T, int) or T < LAST - 2 else 16 * (LAST - 3))
                    STT(y_res, y_res, yrs, g_fin, ALU.mult, ALU.mult).then_inc(y_ready, 1)

            dve.sem_inc(u_free, RING_U)
            expert_steps(dve, group, end, begin, work)

        @block.tensor
        def _(pe):
            def mm(out_, lhsT, rhs, start=True, stop=True):
                return nc.tensor.matmul(out_, lhsT, rhs, start=start, stop=stop, skip_group_check=True)

            pe.wait_ge(fills, FILLS)

            def square_sums(T):
                pe.wait_ge(squared, T + 1)
                wait(pe, rs_ready, T)
                for k in range(KC):
                    last = mm(sum_psum, ones[:, :], sqT[:, k, :], k == 0, k == KC - 1)
                last.then_inc(summed, 1)

            def tile_step(T, p, k):
                lead = isinstance(T, int) and T == 0
                pe.wait_ge(n_ready, T + 1)
                for n, a, w in COLS:
                    if lead and n in ("qs", "so"):
                        continue
                    t = T - 1 if n in ("qs", "so") else T
                    pe.wait_ge(w_landed[n], 16)
                    wait(pe, unit_taken[n], t)
                    if n in ("u", "ks", "qs"):
                        for c in range(4):
                            for kk in range(KC):
                                last = mm(b4(PSUM_OF[n])[:, c, :], w_in_sb[:, kk, a + c * P:a + (c + 1) * P],
                                          nT[p][:, kk, :], kk == 0, kk == KC - 1)
                    else:
                        dst = gate_psum if n == "gates" else bank[PSUM_OF[n]][:, :]
                        for kk in range(KC):
                            last = mm(dst, nT[p][:, kk, :], w_in_sb[:, kk, a:a + w], kk == 0, kk == KC - 1)
                    last.then_inc(unit_done[n], 1)
                    if n == "u" and not (isinstance(T, int) and T == LAST):
                        square_sums(T + 1)

            square_sums(0)
            project(pe, tile_step)

            pe.wait_ge(gate_in, 1)
            pe.wait_ge(unit_taken["u"], TILES)
            mm(bank[2][:, 0:W36], tri, lf).then_inc(gate_pe, 1)
            pe.wait_ge(gate_in, 2)
            pe.wait_ge(unit_taken["qs"], LAST)
            pe.wait_ge(unit_taken["so"], LAST)
            pe.wait_ge(unit_taken["vs"], TILES)
            for T in range(TILES):
                mm(bank[3 + T // 4][0:MH, T % 4 * P:(T % 4 + 1) * P], cols[:, 0, T * MH:(T + 1) * MH], ident[:, :])
            for T in range(TILES):
                last = mm(bank[(6, 7, 2)[T // 4]][0:MH, T % 4 * P:(T % 4 + 1) * P], tmp36[:, T * MH:(T + 1) * MH],
                          ident[:, :])
            last.then_inc(gate_pe, 1)
            pe.wait_ge(unit_taken["gates"], TILES)
            pe.wait_ge(rs_ready, TILES)
            pe.wait_ge(late_in, 16 * N_LATE)
            def fold(a, b):
                for u in range(a, b):
                    j = u // 2
                    pe.wait_ge(w_q_landed[j // (2 * PH // 4)], 16)
                    wait(pe, fold_copied, u - 1)
                    for k in range(KC // 2):
                        last = mm(acc[:, u % 2, k * P:(k + 1) * P],
                                  w_qT[:, j, (u % 2 * 4 + k) * P:(u % 2 * 4 + k + 1) * P], subT[:, j % 2, :])
                    last.then_inc(fold_done, 1)

            fold(*FOLDS[0])
            pe.wait_ge(gate_in, 3)
            for n, rows in enumerate((rows_wi, rows_em, rows_ws)):
                for T in range(TILES):
                    mm(bank[3][:, n * W36 + T * MH:n * W36 + (T + 1) * MH], rows[:, T * P:(T + 1) * P],
                       ident[0:MH, 0:MH])
            mm(bank[4][:, 0:W36], ones[0:MH, :], dec_blk).then_inc(gate_pe, 1)

            def qk(T):
                lead = isinstance(T, int) and T == 0
                pe.wait_ge(mix_in, 32 + 64 * T)
                if lead:
                    pe.wait_ge(gates_ready, 1)
                else:
                    wait(pe, n2_moved, T - 1)
                if not lead:
                    for h in range(MH):
                        mm(b4(2)[:, h, :], w_qk[:, 0, h, :], cT[:, h, :])
                    for h in range(MH):
                        mm(b4(3)[:, h, :], w_qk[:, 1, h, :], cT[:, h, :])
                for h in range(MH):
                    last = mm(b4(4)[:, h, :], cT[:, h, :], w_qk[:, 1, h, :])
                last.then_inc(qk_done, 1)

            def se(T):
                pe.wait_ge(qk_copied, T)
                pe.wait_ge(m_blk_ready, T)
                for h in range(MH):
                    mm(b4(2)[:, h, :], k_m[:, h, :], q_m[:, h, :])
                mm(bank[3][:, :], ones[0:MH, :], m_blk.rearrange("p h t -> p (h t)"), True, False)
                mm(bank[3][:, :], ident_h[:, :], neg_m[:, :].unsqueeze(1).broadcast_to([P, MH, P]), False,
                   True).then_inc(se_done, 1)

            def hh(T):
                pe.wait_ge(p_ready, T)
                pe.wait_ge(kw_ready, T + 1)
                pe.wait_ge(state_ready, T)
                wait(pe, h_ready, T - 1)
                for h in range(MH):
                    mm(b2(4 + h // 2)[:, h % 2, :], wexp[:, h, :], vx[:, h, :])
                for h in range(MH):
                    last = mm(b2(6 + h // 2)[:, h % 2, :], q_m[:, h, :], state[:, h, :])
                last.then_inc(hh_done, 1)
                dstate(T)

            def dstate(T):
                for h in range(MH):
                    last = mm(b2(2 + h // 2)[:, h % 2, :], kw[:, h, :], vx[:, h, :])
                last.then_inc(dstate_done, 1)

            def hn_t(T):
                pe.wait_ge(hn_ready, T)
                for h in range(MH):
                    last = nc.tensor.transpose(b4(4)[:, h, :], hb[:, h, :], ident[:, :])
                last.then_inc(hnT_done, 1)

            def z(T, i):
                c = units_before(T) + i
                pe.wait_ge(k_in, 16 * (c + 1))
                if diagonal(i):
                    pe.wait_ge(state_ready, T + 1)
                    pe.wait_ge(mix_in, 32 + 64 * T)
                wait(pe, a_ready, 2 * c)
                for hg in range(2):
                    r = slice(SD * hg, SD * hg + SD)
                    for cc in range(SHP):
                        last = mm(bank[2 + hg][:, cc * P:(cc + 1) * P], keys[r, cc, :], qsT[r, cc, :], cc == 0,
                                  False)
                    last.then_inc(z_done, 1)

            def s(T, i):
                c = units_before(T) + i
                for hg in range(2):
                    pe.wait_ge(sp_ready, 2 * c + hg + 1)
                    b = bank[2 + hg][:, :]
                    last = mm(b, neg_tri[:, :], sp_[hg], False, False)
                    if diagonal(i):
                        last = mm(b, ident_h[:, :], neg_s[:, :].unsqueeze(1).broadcast_to([P, SHP, P]), False, True)
                    else:
                        if hg == 0:
                            pe.wait_ge(later_ready, c)
                        last = mm(b, ones[:, :], later[hg], False, True)
                    last.then_inc(s_done, 1)

            def av(T, i):
                c = units_before(T) + i
                pe.wait_ge(v_in, 16 * (c + 1))
                for hg in range(2):
                    pe.wait_ge(a_ready, 2 * c + hg + 1)
                    for cc in range(SHP):
                        h = 2 * cc + hg
                        last = mm(bank[5][:, h * SD:(h + 1) * SD], zl[hg][:, cc * P:(cc + 1) * P], vals[:, h, :],
                                  diagonal(i) and h == 0, True)
                last.then_inc(av_done, 1)

            def on_t(T):
                pe.wait_ge(on_ready, T)
                for c in range(4):
                    last = nc.tensor.transpose(b4(2)[:, c, :], on[:, c * P:(c + 1) * P], ident[:, :])
                last.then_inc(onT_done, 1)

            def w_out_part(i):
                def f(T):
                    if i == 0:
                        pe.wait_ge(ym_ready, T)
                        pe.wait_ge(ys_ready, T)
                        pe.wait_ge(w_out_landed, 16)
                        pe.wait_ge(inter_ready, T)
                    n, k0 = i // 2, i % 2 * 4
                    for k in range(k0, k0 + 4):
                        last = mm(bank[(4, 7)[n]][:, :], yT[:, k, :], w_out_sb[:, k, n * 512:(n + 1) * 512], k == 0,
                                  k == KC - 1)
                    if i == 3:
                        last.then_inc(mixed, 1)
                return f

            def n2_t(T):
                pe.wait_ge(n2_ready, T)
                for k in range(KC):
                    last = nc.tensor.transpose(b4(2 + k // 4)[:, k % 4, :], hx[:, k * P:(k + 1) * P],
                                               ident[:, :])
                last.then_inc(n2T_done, 1)

            def n2_rows(T):
                pe.wait_ge(n2T_copied, T)
                for k in range(KC):
                    last = nc.tensor.transpose(b4(2 + k // 4)[:, k % 4, :], n2T[:, k, :], ident[:, :])
                last.then_inc(n2_back, 1)

            def scores(k0, k1):
                def f(T, h, mix):
                    if k0 == 0:
                        pe.wait_ge(n2T_copied, T)
                        pe.wait_ge(fold_copied, 4 * PH)
                        pe.wait_ge(h_ready, T)
                        if mix:
                            pe.wait_ge(inter_ready, T + 1)
                        pe.wait_ge(scores_free, PH * (T - 1) + h + 1)
                    for k in range(k0, k1):
                        last = mm(bank[6][:, 0:2 * NKEY].rearrange("p (j n) -> p j n", j=2), n2T[:, k, :],
                                  w_score[:, bass.ds(2 * h, 2), k, :], k == 0, k == KC - 1)
                    if k1 == KC:
                        last.then_inc(scores_done, 1)
                return f

            work = {
                "mix": {(0, 1): qk, (0, 4): se, (1, 0): hh, (1, 6): hn_t, (2, 0): lambda T: z(T, 0),
                        (2, 4): lambda T: s(T, 0), (2, 7): lambda T: av(T, 0), (11, 4): on_t,
                        (11, 6): w_out_part(0), (12, 0): w_out_part(1), (12, 2): w_out_part(2),
                        (12, 4): w_out_part(3), (13, 5): n2_t, (14, 2): n2_rows},
                "route": {},
                "blocks": {0: z, 4: s, 6: av},
                "heads": {1: scores(0, KC // 2), 2: scores(KC // 2, KC)},
                "fold": fold,
            }

            qk(0)
            pe.wait_ge(kw_ready, 1)
            dstate(0)
            mix_first(work, {(1, 0): FOLDS[1], (2, 0): FOLDS[2], 0: FOLDS[3], (12, 4): FOLDS[4]})

            def begin(T, route, dot, sums):
                if sums:
                    wait(pe, acc_read, T - 2)

            def group(T, g, at_pick, dot, sums):
                b = (T - 2) * GROUPS + g
                for jj in range(GROUP):
                    if sums:
                        pe.wait_ge(diag_ready, b * GROUP + jj + 1)
                        pe.wait_ge(v_landed[jj % RING_V], b * (16 * GROUP // RING_V) + 16 * (jj // RING_V + 1))
                        first = isinstance(g, int) and g == 0 and jj == 0
                        final = isinstance(g, int) and g == GROUPS - 1 and jj == GROUP - 1
                        for n in range(2):
                            last = mm(acc[:, n, :], diag[:, jj % 4, :], ring_v[:, jj % RING_V, n * 512:(n + 1) * 512],
                                      first, final)
                        last.then_inc(v_free, 1)
                    for f in at_pick.get(jj, ()):
                        f()

            pe.sem_inc(v_free, RING_V)
            expert_steps(pe, group, lambda T, dot, sums: None, begin, work)


_ARGS = ["xT", "xn_in", "w_in", "w_out", "w_queryT", "sub_t", "mlstm_w", "gain_cols", "g_final",
         "gate_bias", "expert_u", "expert_v"]


def kernel(x, meta, norm_mix_g, w_in, conv_w, conv_b, w_qm, w_km, b_i, b_f, mlstm_skip, mlstm_gn_g,
           sb_norm_g, w_out, norm_ffn_g, w_query, sub_keys, expert_u, expert_v, norm_final_g):
    import numpy as np
    import concourse.bacc as bacc
    from concourse.bass_utils import run_bass_kernel_spmd

    def cols(a):
        return np.asarray(a).reshape(-1, P).T

    x, meta = np.asarray(x), np.asarray(meta)
    rows = np.concatenate([np.zeros((P - N_META, D), x.dtype), meta, x[0]], axis=0)
    taps = np.asarray(conv_w)[0].reshape(CONV, MH, P).transpose(2, 1, 0).reshape(P, MH * CONV)
    arrays = {
        "xT": rows.T,
        "xn_in": rows,
        "w_in": np.asarray(w_in)[0],
        "w_out": np.asarray(w_out)[0],
        "w_queryT": np.asarray(w_query)[0].T,
        "sub_t": np.asarray(sub_keys)[0].transpose(2, 0, 1),
        "mlstm_w": np.stack([np.asarray(w_qm)[0], np.asarray(w_km)[0]]).transpose(2, 0, 1, 3),
        "gain_cols": np.concatenate([cols(norm_mix_g), cols(mlstm_gn_g), cols(mlstm_skip), cols(sb_norm_g), taps,
                                     cols(conv_b), cols(norm_ffn_g)], axis=1),
        "g_final": np.asarray(norm_final_g)[None],
        "gate_bias": np.concatenate([np.asarray(b_i), np.asarray(b_f)], axis=1),
        "expert_u": np.asarray(expert_u)[0],
        "expert_v": np.asarray(expert_v)[0],
    }
    nc = bacc.Bacc("TRN2", target_bir_lowering=False, num_devices=1)
    arrays = {n: np.ascontiguousarray(a) for n, a in arrays.items()}
    args = [nc.dram_tensor(n, arrays[n].shape, F32, kind="ExternalInput").ap() for n in _ARGS]
    args.append(nc.dram_tensor("out", (SEQ, D), F32, kind="ExternalOutput").ap())
    program(nc, *args)
    r = run_bass_kernel_spmd(nc, [arrays], core_ids=[0])
    return r.results[0]["out"].reshape(1, SEQ, D)
```
